# Optimizing a Trainium2 kernel written in Bass

```python
import math
import jax, jax.numpy as jnp
from jax import lax
import numpy as np

D_MODEL = 2048
BATCH = 1
SEQ = 512
DEPTH = 1

D_M = D_MODEL
N_M_HEADS = 8
M_V_DIM = D_M // N_M_HEADS
M_QK_DIM = M_V_DIM // 2
D_QK = N_M_HEADS * M_QK_DIM
D_G = D_MODEL
N_G_HEADS = 8
G_DIM = D_G // N_G_HEADS
D_MIX = D_M + D_G
CHUNK = 128
CONV_W = 4
EPS = 1e-6

COL_SIZES = (D_QK, D_QK, D_M, D_M, D_M, N_M_HEADS, N_M_HEADS, D_G, D_G, D_G)
D_IN = sum(COL_SIZES)


def _rmsnorm(x, w):
    xf = x.astype(jnp.float32)
    r = xf * lax.rsqrt(jnp.mean(xf * xf, axis=-1, keepdims=True) + EPS)
    return (r * w.astype(jnp.float32)).astype(x.dtype)

def _split_cols(h):
    offs = np.cumsum((0,) + COL_SIZES)
    return [h[..., int(offs[i]):int(offs[i + 1])] for i in range(len(COL_SIZES))]

def _causal_depthwise_conv(x, w, b):
    S = x.shape[1]
    xp = jnp.pad(x, ((0, 0), (CONV_W - 1, 0), (0, 0)))
    y = b
    for j in range(CONV_W):
        y = y + w[j] * lax.dynamic_slice_in_dim(xp, j, S, axis=1)
    return y

def _mlstm_chunkwise(q, k, v, log_i, log_f):
    B, S, H, DK = q.shape
    DV = v.shape[-1]
    NC = S // CHUNK

    def to_chunks(a):
        a = a.reshape((B, NC, CHUNK, H) + a.shape[3:])
        perm = (1, 0, 3, 2) + tuple(range(4, a.ndim))
        return a.transpose(perm)

    qc, kc, vc = to_chunks(q), to_chunks(k), to_chunks(v)
    lic, lfc = to_chunks(log_i), to_chunks(log_f)
    causal = jnp.tril(jnp.ones((CHUNK, CHUNK), dtype=bool))

    def step(carry, inp):
        C, n, m = carry
        qb, kb, vb, li, lf = inp
        b = jnp.cumsum(lf, axis=-1)
        D = b[..., :, None] - b[..., None, :] + li[..., None, :]
        D = jnp.where(causal, D, -jnp.inf)
        inter = b + m[..., None]
        m_t = jnp.maximum(inter, jnp.max(D, axis=-1))
        decay = jnp.exp(inter - m_t)
        P = jnp.exp(D - m_t[..., None])
        Sqk = jnp.einsum('bhtd,bhsd->bhts', qb, kb) * P
        num = jnp.einsum('bhts,bhsv->bhtv', Sqk, vb) + decay[..., None] * jnp.einsum('bhtd,bhdv->bhtv', qb, C)
        den = jnp.sum(Sqk, axis=-1) + decay * jnp.einsum('bhtd,bhd->bht', qb, n)
        h = num / jnp.maximum(jnp.abs(den), jnp.exp(-m_t))[..., None]
        bL = b[..., -1]
        wlog = bL[..., None] - b + li
        m_new = jnp.maximum(bL + m, jnp.max(wlog, axis=-1))
        a = jnp.exp(bL + m - m_new)
        ws = jnp.exp(wlog - m_new[..., None])
        C_new = a[..., None, None] * C + jnp.einsum('bhs,bhsd,bhsv->bhdv', ws, kb, vb)
        n_new = a[..., None] * n + jnp.einsum('bhs,bhsd->bhd', ws, kb)
        return (C_new, n_new, m_new), h

    init = (jnp.zeros((B, H, DK, DV), jnp.float32),
            jnp.zeros((B, H, DK), jnp.float32),
            jnp.zeros((B, H), jnp.float32))
    _, hc = lax.scan(step, init, (qc, kc, vc, lic, lfc))
    return hc.transpose(1, 0, 3, 2, 4).reshape(B, S, H, DV)

def _layernorm(x, w, b):
    xf = x.astype(jnp.float32)
    mu = jnp.mean(xf, axis=-1, keepdims=True)
    var = jnp.mean(jnp.square(xf - mu), axis=-1, keepdims=True)
    return (xf - mu) * lax.rsqrt(var + EPS) * w + b

def first_inputs(seed: int = 0) -> dict:
    key = jax.random.key(seed)
    ks = jax.random.split(key, 14)
    f32 = jnp.float32
    x = jax.random.normal(ks[0], (BATCH, SEQ, D_MODEL), f32)
    norm_w = 1.0 + 0.02 * jax.random.normal(ks[1], (D_MODEL,), f32)
    w_in = jax.random.normal(ks[2], (D_MODEL, D_IN), f32) * D_MODEL ** -0.5
    conv_w = jax.random.normal(ks[3], (CONV_W, 2 * D_QK), f32) * CONV_W ** -0.5
    conv_b = 0.02 * jax.random.normal(ks[4], (2 * D_QK,), f32)
    b_igate = 0.1 * jax.random.normal(ks[5], (N_M_HEADS,), f32)
    b_fgate = 3.0 + 3.0 * jax.random.uniform(ks[6], (N_M_HEADS,), f32)
    mlstm_norm_w = 1.0 + 0.02 * jax.random.normal(ks[7], (D_M,), f32)
    sgu_norm_w = 1.0 + 0.02 * jax.random.normal(ks[8], (D_G,), f32)
    sgu_norm_b = 0.02 * jax.random.normal(ks[9], (D_G,), f32)
    w_spatial = jax.random.normal(ks[10], (N_G_HEADS, CHUNK, CHUNK), f32) * CHUNK ** -0.5
    b_spatial = 1.0 + 0.1 * jax.random.normal(ks[11], (N_G_HEADS, CHUNK), f32)
    w_out = jax.random.normal(ks[12], (D_MIX, D_MODEL), f32) * D_MIX ** -0.5
    final_norm_w = 1.0 + 0.02 * jax.random.normal(ks[13], (D_MODEL,), f32)
    return {"x": x, "norm_w": norm_w, "w_in": w_in, "conv_w": conv_w, "conv_b": conv_b,
            "b_igate": b_igate, "b_fgate": b_fgate, "mlstm_norm_w": mlstm_norm_w,
            "sgu_norm_w": sgu_norm_w, "sgu_norm_b": sgu_norm_b, "w_spatial": w_spatial,
            "b_spatial": b_spatial, "w_out": w_out, "final_norm_w": final_norm_w}

def first_block(x, norm_w, w_in, conv_w, conv_b, b_igate, b_fgate, mlstm_norm_w,
              sgu_norm_w, sgu_norm_b, w_spatial, b_spatial, w_out, final_norm_w):
    B, S, _ = x.shape
    NC = S // CHUNK
    f32 = jnp.float32
    h = x
    for _layer in range(DEPTH):
        xn = _rmsnorm(h, norm_w)
        proj = jnp.einsum('bsd,de->bse', xn, w_in).astype(f32)
        q, k, v_m, o_m, z_m, i_pre, f_pre, u_g, v_g, z_g = _split_cols(proj)

        qk = jax.nn.silu(_causal_depthwise_conv(jnp.concatenate([q, k], axis=-1),
                                                 conv_w.astype(f32), conv_b.astype(f32)))
        q = qk[..., :D_QK].reshape(B, S, N_M_HEADS, M_QK_DIM)
        k = qk[..., D_QK:].reshape(B, S, N_M_HEADS, M_QK_DIM) * (M_QK_DIM ** -0.5)
        v = v_m.reshape(B, S, N_M_HEADS, M_V_DIM)
        log_i = i_pre + b_igate.astype(f32)
        log_f = jax.nn.log_sigmoid(f_pre + b_fgate.astype(f32))
        hm = _mlstm_chunkwise(q, k, v, log_i, log_f)
        hm = hm * lax.rsqrt(jnp.mean(hm * hm, axis=-1, keepdims=True) + EPS)
        hm = hm.reshape(B, S, D_M) * mlstm_norm_w.astype(f32)
        y_m = hm * jax.nn.sigmoid(o_m) * jax.nn.silu(z_m)

        u = jax.nn.gelu(u_g)
        vg = jax.nn.gelu(v_g).reshape(B, S, N_G_HEADS, G_DIM)
        vg = _layernorm(vg, sgu_norm_w.reshape(N_G_HEADS, G_DIM).astype(f32),
                        sgu_norm_b.reshape(N_G_HEADS, G_DIM).astype(f32))
        vg = vg.reshape(B, NC, CHUNK, N_G_HEADS, G_DIM)
        w_s = jnp.where(jnp.tril(jnp.ones((CHUNK, CHUNK), dtype=bool)), w_spatial.astype(f32), 0.0)
        sv = jnp.einsum('hts,bnshc->bnthc', w_s, vg) + b_spatial.astype(f32).T[None, None, :, :, None]
        y_g = u * sv.reshape(B, S, D_G) * jax.nn.silu(z_g)

        y = jnp.concatenate([y_m, y_g], axis=-1).astype(x.dtype)
        h = h + jnp.einsum('bse,ed->bsd', y, w_out)
    return _rmsnorm(h, final_norm_w)


_first_inputs = first_inputs


def first_inputs(seed=0):
    import zlib

    import numpy as np

    out = dict(_first_inputs(seed))
    spreads = {}
    factors = {'norm_w': 4.092,
     'conv_b': 64.0,
     'b_igate': 200.0,
     'mlstm_norm_w': 200.0,
     'sgu_norm_w': 100.28,
     'sgu_norm_b': 95.777,
     'final_norm_w': 21.333,
     'b_spatial': 12.122}
    for name, (base, spread) in spreads.items():
        noise = np.random.default_rng([zlib.crc32(name.encode()), seed]).standard_normal(out[name].shape)
        drawn = base * np.exp(spread * noise) if base else spread * noise
        out[name] = __import__('jax').numpy.asarray(drawn.astype(out[name].dtype))
    for name, factor in factors.items():
        out[name] = (out[name] * factor).astype(out[name].dtype)
    return out


_narrow_inputs = first_inputs


def first_inputs(seed=0):

    out = dict(_narrow_inputs(seed))
    wider = {'mlstm_norm_w': 5.66,
     'sgu_norm_w': 4.07,
     'sgu_norm_b': 4.06,
     'b_spatial': 3.93,
     'final_norm_w': 3.12}
    for name, times in wider.items():
        mean = out[name].mean()
        out[name] = (mean + times * (out[name] - mean)).astype(out[name].dtype)
    return out


DEPTH_2 = 2

N_META = 16
D_MIX_2 = D_MODEL
CONV_W_2 = D_MIX_2 // 4
CONV_K = 31
HEAD_DIM = 64
N_HEADS = (D_MIX_2 // 2) // HEAD_DIM
N_KV = 4
GROUP = N_HEADS // N_KV
ATT_W = N_HEADS * HEAD_DIM
KV_W = N_KV * HEAD_DIM
WINDOW = 128
BLOCK = 128
ROT_DIM = HEAD_DIM // 4
ROPE_THETA = 500000.0
LRU_W = D_MIX_2 // 4
LRU_HEADS = 8
LRU_HEAD_DIM = LRU_W // LRU_HEADS
LRU_CONV_K = 4
LRU_C = 8.0
IN_WIDTHS = (CONV_W_2, CONV_W_2, CONV_W_2,
             ATT_W, KV_W, KV_W, ATT_W,
             LRU_W, LRU_W)
IN_TOTAL = sum(IN_WIDTHS)
OUT_IN = CONV_W_2 + ATT_W + LRU_W
LN_EPS = 1e-5
DEEPNORM_ALPHA = (2.0 * DEPTH_2) ** 0.25
DEEPNORM_BETA = (8.0 * DEPTH_2) ** -0.25
NEG_INF = -1e30


def _layer_norm(x, g, b):
    xf = x.astype(jnp.float32)
    mu = jnp.mean(xf, axis=-1, keepdims=True)
    var = jnp.mean(jnp.square(xf - mu), axis=-1, keepdims=True)
    y = (xf - mu) * lax.rsqrt(var + LN_EPS)
    return (y * g.astype(jnp.float32) + b.astype(jnp.float32)).astype(x.dtype)

def _causal_depthwise_conv_2(x, w, b):
    k = w.shape[0]
    y = lax.conv_general_dilated(
        x, w[:, None, :].astype(x.dtype), window_strides=(1,), padding=[(k - 1, 0)],
        dimension_numbers=("NWC", "WIO", "NWC"), feature_group_count=x.shape[-1])
    return y + b

def _partial_rotary(x, pos):
    half = ROT_DIM // 2
    inv_freq = ROPE_THETA ** (-jnp.arange(half, dtype=jnp.float32) / half)
    ang = pos.astype(jnp.float32)[:, None] * inv_freq[None, :]
    cos = jnp.cos(ang)[None, :, None, :]
    sin = jnp.sin(ang)[None, :, None, :]
    x1 = x[..., :half].astype(jnp.float32)
    x2 = x[..., half:ROT_DIM].astype(jnp.float32)
    rot = jnp.concatenate([x1 * cos - x2 * sin, x2 * cos + x1 * sin], axis=-1).astype(x.dtype)
    return jnp.concatenate([rot, x[..., ROT_DIM:]], axis=-1)

def _sliding_window_sink_attention(q, k, v, sinks):
    B, L, H, Dh = q.shape
    S = L - N_META
    nblk = S // BLOCK
    scale = Dh ** -0.5
    sink_kg = sinks.astype(jnp.float32).reshape(N_KV, GROUP)

    qm, qr = q[:, :N_META], q[:, N_META:]
    km, kr = k[:, :N_META], k[:, N_META:]
    vm, vr = v[:, :N_META], v[:, N_META:]

    qb = qr.reshape(B, nblk, BLOCK, N_KV, GROUP, Dh)
    kb = kr.reshape(B, nblk, BLOCK, N_KV, Dh)
    vb = vr.reshape(B, nblk, BLOCK, N_KV, Dh)
    pad = ((0, 0), (1, 0), (0, 0), (0, 0), (0, 0))
    k_band = jnp.concatenate([jnp.pad(kb, pad)[:, :-1], kb], axis=2)
    v_band = jnp.concatenate([jnp.pad(vb, pad)[:, :-1], vb], axis=2)

    s_meta = jnp.einsum("bnqkgd,bmkd->bkgnqm", qb, km).astype(jnp.float32) * scale
    s_band = jnp.einsum("bnqkgd,bnjkd->bkgnqj", qb, k_band).astype(jnp.float32) * scale
    qi = jnp.arange(BLOCK)[:, None]
    kj = jnp.arange(2 * BLOCK)[None, :]
    diff = BLOCK + qi - kj
    in_window = (diff >= 0) & (diff < WINDOW)
    blk = jnp.arange(nblk)[:, None, None]
    valid = in_window[None] & ((kj[None] >= BLOCK) | (blk > 0))
    s_band = jnp.where(valid[None, None, None], s_band, NEG_INF)
    sink_col = jnp.broadcast_to(sink_kg[None, :, :, None, None, None], s_meta.shape[:-1] + (1,))
    probs = jax.nn.softmax(jnp.concatenate([s_meta, s_band, sink_col], axis=-1), axis=-1)
    p_meta = probs[..., :N_META].astype(v.dtype)
    p_band = probs[..., N_META:N_META + 2 * BLOCK].astype(v.dtype)
    out_r = (jnp.einsum("bkgnqm,bmkd->bnqkgd", p_meta, vm)
             + jnp.einsum("bkgnqj,bnjkd->bnqkgd", p_band, v_band)).reshape(B, S, H, Dh)

    qmg = qm.reshape(B, N_META, N_KV, GROUP, Dh)
    s_mm = jnp.einsum("bqkgd,bmkd->bkgqm", qmg, km).astype(jnp.float32) * scale
    causal = jnp.tril(jnp.ones((N_META, N_META), dtype=bool))
    s_mm = jnp.where(causal[None, None, None], s_mm, NEG_INF)
    sink_mm = jnp.broadcast_to(sink_kg[None, :, :, None, None], s_mm.shape[:-1] + (1,))
    p_mm = jax.nn.softmax(jnp.concatenate([s_mm, sink_mm], axis=-1), axis=-1)[..., :N_META]
    out_m = jnp.einsum("bkgqm,bmkd->bqkgd", p_mm.astype(v.dtype), vm).reshape(B, N_META, H, Dh)

    return jnp.concatenate([out_m, out_r], axis=1)

def _rg_lru(x, w_a, b_a, w_x, b_x, lam):
    B, L, C = x.shape
    xh = x.reshape(B, L, LRU_HEADS, LRU_HEAD_DIM)
    r = jax.nn.sigmoid(jnp.einsum("blhi,hij->blhj", xh, w_a).reshape(B, L, C) + b_a)
    i = jax.nn.sigmoid(jnp.einsum("blhi,hij->blhj", xh, w_x).reshape(B, L, C) + b_x)
    log_a = -LRU_C * r.astype(jnp.float32) * jax.nn.softplus(-lam.astype(jnp.float32))
    a = jnp.exp(log_a)
    u = jnp.sqrt(-jnp.expm1(2.0 * log_a)) * (i * x).astype(jnp.float32)

    def combine(c1, c2):
        a1, b1 = c1
        a2, b2 = c2
        return a1 * a2, a2 * b1 + b2

    _, h = lax.associative_scan(combine, (a, u), axis=1)
    return h.astype(x.dtype)

def _hybrid_layer(h, pos, w_in, conv_dw_w, conv_dw_b, conv_ln_g, conv_ln_b, conv_pw_w, conv_pw_b,
                  attn_sinks, lru_conv_w, lru_conv_b, lru_wa, lru_ba, lru_wx, lru_bx, lru_lambda,
                  w_out, ln_post_g, ln_post_b):
    B, L, _ = h.shape
    proj = h @ w_in
    split_pts = [int(s) for s in np.cumsum(IN_WIDTHS)[:-1]]
    (c_val, c_glu, c_gate, q, k, v, a_gate, r_x, r_gate) = jnp.split(proj, split_pts, axis=-1)

    c = c_val * jax.nn.sigmoid(c_glu)
    c = _causal_depthwise_conv_2(c, conv_dw_w, conv_dw_b)
    c = jax.nn.silu(_layer_norm(c, conv_ln_g, conv_ln_b))
    c = c @ conv_pw_w + conv_pw_b
    y_conv = c * jax.nn.silu(c_gate)

    q = _partial_rotary(q.reshape(B, L, N_HEADS, HEAD_DIM), pos)
    k = _partial_rotary(k.reshape(B, L, N_KV, HEAD_DIM), pos)
    v = v.reshape(B, L, N_KV, HEAD_DIM)
    att = _sliding_window_sink_attention(q, k, v, attn_sinks).reshape(B, L, ATT_W)
    y_attn = att * jax.nn.silu(a_gate)

    r = _causal_depthwise_conv_2(r_x, lru_conv_w, lru_conv_b)
    r = _rg_lru(r, lru_wa, lru_ba, lru_wx, lru_bx, lru_lambda)
    y_lru = r * jax.nn.silu(r_gate)

    mixed = jnp.concatenate([y_conv, y_attn, y_lru], axis=-1) @ w_out
    return _layer_norm(DEEPNORM_ALPHA * h + mixed, ln_post_g, ln_post_b)

def second_inputs(seed: int = 0) -> dict:
    key = jax.random.key(seed)
    ks = jax.random.split(key, 24)
    f32 = jnp.float32
    nrm = lambda k, shape, s: jax.random.normal(k, shape, f32) * s
    u = jax.random.uniform(ks[17], (DEPTH_2, LRU_W), f32, 0.9, 0.999)
    s = u ** (1.0 / LRU_C)
    lam = jnp.log(s) - jnp.log1p(-s)
    return {
        "x": nrm(ks[0], (BATCH, SEQ, D_MODEL), 1.0),
        "meta_tokens": nrm(ks[1], (N_META, D_MODEL), 1.0),
        "ln_in_g": 1.0 + nrm(ks[2], (D_MODEL,), 0.02),
        "ln_in_b": nrm(ks[3], (D_MODEL,), 0.02),
        "w_in": nrm(ks[4], (DEPTH_2, D_MODEL, IN_TOTAL), D_MODEL ** -0.5),
        "conv_dw_w": nrm(ks[5], (DEPTH_2, CONV_K, CONV_W_2), CONV_K ** -0.5),
        "conv_dw_b": nrm(ks[6], (DEPTH_2, CONV_W_2), 0.01),
        "conv_ln_g": 1.0 + nrm(ks[7], (DEPTH_2, CONV_W_2), 0.02),
        "conv_ln_b": nrm(ks[8], (DEPTH_2, CONV_W_2), 0.02),
        "conv_pw_w": nrm(ks[9], (DEPTH_2, CONV_W_2, CONV_W_2), DEEPNORM_BETA * CONV_W_2 ** -0.5),
        "conv_pw_b": nrm(ks[10], (DEPTH_2, CONV_W_2), 0.01),
        "attn_sinks": nrm(ks[11], (DEPTH_2, N_HEADS), 0.5),
        "lru_conv_w": nrm(ks[12], (DEPTH_2, LRU_CONV_K, LRU_W), LRU_CONV_K ** -0.5),
        "lru_conv_b": nrm(ks[13], (DEPTH_2, LRU_W), 0.01),
        "lru_wa": nrm(ks[14], (DEPTH_2, LRU_HEADS, LRU_HEAD_DIM, LRU_HEAD_DIM), LRU_HEAD_DIM ** -0.5),
        "lru_ba": nrm(ks[15], (DEPTH_2, LRU_W), 0.01),
        "lru_wx": nrm(ks[16], (DEPTH_2, LRU_HEADS, LRU_HEAD_DIM, LRU_HEAD_DIM), LRU_HEAD_DIM ** -0.5),
        "lru_bx": nrm(ks[18], (DEPTH_2, LRU_W), 0.01),
        "lru_lambda": lam,
        "w_out": nrm(ks[19], (DEPTH_2, OUT_IN, D_MODEL), DEEPNORM_BETA * OUT_IN ** -0.5),
        "ln_post_g": 1.0 + nrm(ks[20], (DEPTH_2, D_MODEL), 0.02),
        "ln_post_b": nrm(ks[21], (DEPTH_2, D_MODEL), 0.02),
    }

def second_block(x, meta_tokens, ln_in_g, ln_in_b, w_in, conv_dw_w, conv_dw_b, conv_ln_g, conv_ln_b,
              conv_pw_w, conv_pw_b, attn_sinks, lru_conv_w, lru_conv_b, lru_wa, lru_ba, lru_wx,
              lru_bx, lru_lambda, w_out, ln_post_g, ln_post_b):
    B = x.shape[0]
    meta = jnp.broadcast_to(meta_tokens[None].astype(x.dtype), (B, N_META, x.shape[-1]))
    h = jnp.concatenate([meta, x], axis=1)
    h = _layer_norm(h, ln_in_g, ln_in_b)
    pos = jnp.arange(h.shape[1], dtype=jnp.int32)
    for l in range(DEPTH_2):
        h = _hybrid_layer(h, pos, w_in[l], conv_dw_w[l], conv_dw_b[l], conv_ln_g[l], conv_ln_b[l],
                          conv_pw_w[l], conv_pw_b[l], attn_sinks[l], lru_conv_w[l], lru_conv_b[l],
                          lru_wa[l], lru_ba[l], lru_wx[l], lru_bx[l], lru_lambda[l],
                          w_out[l], ln_post_g[l], ln_post_b[l])
    return h[:, N_META:]


def setup_inputs(seed=0):
    out = dict(first_inputs(seed))
    for name, value in second_inputs(seed + 1).items():
        if name != "x":
            out[name + "_2"] = value
    return out


def reference(
    x, norm_w, w_in, conv_w, conv_b, b_igate, b_fgate, mlstm_norm_w, sgu_norm_w, sgu_norm_b,
    w_spatial, b_spatial, w_out, final_norm_w, meta_tokens_2, ln_in_g_2, ln_in_b_2, w_in_2,
    conv_dw_w_2, conv_dw_b_2, conv_ln_g_2, conv_ln_b_2, conv_pw_w_2, conv_pw_b_2, attn_sinks_2,
    lru_conv_w_2, lru_conv_b_2, lru_wa_2, lru_ba_2, lru_wx_2, lru_bx_2, lru_lambda_2, w_out_2,
    ln_post_g_2, ln_post_b_2,
):
    x = first_block(
        x, norm_w, w_in, conv_w, conv_b, b_igate, b_fgate, mlstm_norm_w, sgu_norm_w, sgu_norm_b,
        w_spatial, b_spatial, w_out, final_norm_w,
    )
    return second_block(
        x, meta_tokens_2, ln_in_g_2, ln_in_b_2, w_in_2, conv_dw_w_2, conv_dw_b_2, conv_ln_g_2,
        conv_ln_b_2, conv_pw_w_2, conv_pw_b_2, attn_sinks_2, lru_conv_w_2, lru_conv_b_2,
        lru_wa_2, lru_ba_2, lru_wx_2, lru_bx_2, lru_lambda_2, w_out_2, ln_post_g_2, ln_post_b_2,
    )


_drawn_inputs = setup_inputs


def setup_inputs(seed=0):
    import zlib

    import numpy as np

    out = dict(_drawn_inputs(seed))
    spreads = {}
    factors = {'ln_in_g_2': 2.855,
     'conv_dw_b_2': 8.0,
     'conv_ln_g_2': 52.567,
     'conv_ln_b_2': 53.044,
     'conv_pw_b_2': 38.531,
     'attn_sinks_2': 47.819,
     'lru_conv_b_2': 7.919,
     'lru_ba_2': 196.26,
     'lru_bx_2': 64.0,
     'ln_in_b_2': 3.76}
    for name, (base, spread) in spreads.items():
        noise = np.random.default_rng([zlib.crc32(name.encode()), seed]).standard_normal(out[name].shape)
        drawn = base * np.exp(spread * noise) if base else spread * noise
        out[name] = __import__('jax').numpy.asarray(drawn.astype(out[name].dtype))
    for name, factor in factors.items():
        out[name] = (out[name] * factor).astype(out[name].dtype)
    return out
```

```python
from contextlib import ExitStack

import numpy as np

import concourse.bass as bass
from concourse import mybir

F32 = mybir.dt.float32
F32R = mybir.dt.float32r
ACT = mybir.ActivationFunctionType
ALU = mybir.AluOpType
AX = mybir.AxisListType
ds = bass.ds

P = 128
D = 2048
KT = D // P
S = 512
ST = S // P
H = 8
DV = D // H
QK = H * P
EPS = 1e-6
C_Q, C_K = 0, QK
C_V, C_O, C_Z = 2 * QK, 2 * QK + D, 2 * QK + 2 * D
C_I = 2 * QK + 3 * D
C_F = C_I + H
C_U = C_F + H
C_VG, C_ZG = C_U + D, C_U + 2 * D

NM = 16
L = NM + S
LH = L // 2
LAYERS = 2
CW = D // 4
CT = CW // P
TAPS = 31
HD = 64
NKV = 4
GROUP = 4
NH = NKV * GROUP
BLK = 128
LN_EPS = 1e-5
ALPHA = (2.0 * LAYERS) ** 0.25
RTAPS = 4
D_CV, D_CG, D_CGATE = 0, CW, 2 * CW
D_Q = 3 * CW
D_K = D_Q + NH * HD
D_V = D_K + NKV * HD
D_AG = D_V + NKV * HD
D_RX = D_AG + NH * HD
D_RG = D_RX + CW

U_GATE = 0
U_SGU = 1
U_MLSTM = U_SGU + 3 * H
U_OUT_M = U_MLSTM + 4 * H
U_OUT_G = U_OUT_M + 8
U_LAYER = U_OUT_G + 8
N_LAYER = 29
O_K, O_V, O_GRP, O_CG, O_PW, O_OUT = 0, 1, 2, 18, 20, 21

K_IDENT, K_ONES, K_TRI, K_ROT = 0, P, 2 * P, 3 * P
K_MASK0 = 4 * P
K_MASK = K_MASK0 + NM + BLK
K_CAUS = K_MASK + NM + 2 * BLK
K_COS = K_CAUS + NM
K_SIN = K_COS + L
K_ALL = K_SIN + L

PR_NORM, PR_CONVW, PR_CONVB, PR_MNORM, PR_FINAL = 0, 16, 80, 96, 112
PR_SGUW, PR_SGUB, PR_LNG, PR_LNB = 128, 144, 160, 176
PL_DW, PL_DWB = 0, TAPS * CT
PL_CLG, PL_CLB, PL_PWB = 128, 132, 136
PL_RW, PL_RB, PL_BA, PL_BX, PL_LAM = 140, 156, 160, 164, 168
PL_PG, PL_PB = 172, 188
PL_END = 204
ROWS1, ROWS_L2 = 64, PL_END - P

LOG1P = [1.0 / (2 * n + 1) for n in range(9)]


def program(nc, a, out):
    consts = a["shape_constants"]
    x_t = nc.dram_tensor("x_feature_major", (P, KT, S), F32, kind="Internal").ap()
    gate_rows = nc.dram_tensor("gate_rows", (H, 2, S), F32, kind="Internal").ap()

    w_in = a["w_in"].rearrange("(k p) n -> p k n", p=P)
    w_out = a["w_out"].rearrange("(k p) n -> p k n", p=P)
    w_in2 = a["w_in_2"].rearrange("l (k p) n -> p (l k) n", p=P)
    w_out2 = a["w_out_2"].rearrange("l (k p) n -> p (l k) n", p=P)
    w_pw = a["conv_pw_w_2"].rearrange("l (k p) n -> p (l k) n", p=P)
    x_nat = a["x"].rearrange("o (i p) d -> p (o i) d", p=P)
    out_nat = out.rearrange("o (i p) d -> p (o i) d", p=P)

    with ExitStack() as ctx:
        base = (nc.sbuf_base + 31) // 32 * 32
        limit = nc.sbuf_top

        class Region:
            def __init__(self, at):
                self.at = at

            def take(self, name, shape, dt=F32):
                size = 4
                for n in shape[1:]:
                    size *= n
                t = nc.alloc_sbuf_tensor_at(name, shape, dt, offset=self.at)
                self.at += (size + 31) // 32 * 32
                assert self.at <= limit, (name, self.at - limit)
                return t

        r0 = Region(base)
        ps = ctx.enter_context(nc.psum_tensor("ps", [P, 8, 512], F32))
        xh = r0.take("x_high", [P, KT, L], F32R)
        xl = r0.take("x_low", [P, KT, L], F32R)
        wh = r0.take("w_high", [P, 4, 4, 256], F32R)
        wl = r0.take("w_low", [P, 4, 4, 256], F32R)
        raw = r0.take("w_raw", [P, 4, 4, 256])
        ident = r0.take("ident", [P, P])
        ones = r0.take("ones", [P, P])
        tri_at = r0.at
        tri = r0.take("tri", [P, P])
        par = r0.take("par", [P, 2, P])
        pl = nc.alloc_sbuf_tensor_at("par_layer", [P, 2, P], F32, offset=r0.at - 2 * P * 4)
        small = r0.take("small", [P, 64])
        at = r0.take("a_t", [P, ST, H])
        big = r0.at

        r1 = Region(big)
        yg = r1.take("y_g", [P, KT, S])
        ym_at = r1.at
        ym = r1.take("y_m", [P, KT, S])
        acc = nc.alloc_sbuf_tensor_at("acc", [P, KT, S], F32, offset=ym_at)
        work = r1.at
        xs = nc.alloc_sbuf_tensor_at("x_scaled", [P, ST, D], F32, offset=big)
        xn = nc.alloc_sbuf_tensor_at("x_natural", [P, ST, D], F32, offset=ym_at)
        rp = Region(work)
        stage = rp.take("x_stage", [P, 4, S])
        prow = rp.take("par_rows", [P, 2, P])
        ra = Region(ym_at)
        ws = ra.take("w_spatial_natural", [P, H, P])
        wst = ra.take("w_spatial_t", [P, H, P])
        rsb = ra.take("w_spatial_rowsum", [P, H, P])
        bsp = ra.take("b_spatial_bc", [P, H, P])
        svr = ra.take("sgu_bias", [P, 2, P])
        sv = ra.take("sgu_v", [P, 2, S])
        li = ra.take("log_i", [8, S])
        xf = ra.take("f_pre", [8, S])
        gz = ra.take("gate_z", [8, S])
        gw = ra.take("gate_w", [8, S])
        gq = ra.take("gate_q", [8, S])
        assert ra.at <= work
        rb = Region(work)
        vg = rb.take("v_gelu", [P, ST, DV])
        vn = rb.take("v_normed", [P, ST, DV])
        ug = rb.take("u_gelu", [P, 2, S])
        zg = rb.take("z_silu_g", [P, 2, S])
        gp = rb.take("gate_p", [8, S])
        gout = rb.take("gate_out", [8, 2, S])
        rc = Region(work)
        qc = rc.take("q_head", [P, S])
        kc = rc.take("k_head", [P, S])
        vv = rc.take("v_head", [P, ST, DV])
        og = rc.take("o_gate", [P, 2, S])
        zz = rc.take("z_silu_m", [P, S])
        bc = rc.take("gate_bc", [P, 2, S])
        pj_at = rc.at
        pj = rc.take("p_tiles", [P, 5 * 256])
        sq = nc.alloc_sbuf_tensor_at("square", [P, 2, S], F32, offset=pj_at)
        rd = nc.alloc_sbuf_tensor_at("recip_bc", [P, S], F32, offset=rc.at)
        cr = rc.take("conv_raw", [P, 4 + S])
        PTAPS = 9
        POFF = [0, 512, 896, 1152]
        ro = Region(work)
        tmp = ro.take("out_tmp", [P, 2, S])
        sqs = ro.take("square_sum", [P, S])
        sqt = ro.take("square_tile", [P, S])
        rb1 = ro.take("rms_bc", [P, S])
        mnat = ro.take("meta_natural", [NM, D])

        r2 = Region(big)
        res = r2.take("residual", [P, KT, L])
        y2_at = r2.at
        y2 = r2.take("y_layer", [P, KT, L])
        work2 = r2.at
        rr = Region(big)
        krw = nc.alloc_sbuf_tensor_at("k_raw", [P, 2, L], F32, offset=big)
        qrw = rr.take("q_raw", [P, 2, L])
        krd = rr.take("k_raw_twice", [P, NKV, L])
        v2 = rr.take("v_tokens", [P, ST + 1, NKV * HD])
        qg = rr.take("q_group", [P, 2, L])
        kg = rr.take("k_group", [P, L])
        vgr = rr.take("v_group", [P, ST + 1, HD])
        shape_at = rr.at
        kshape = rr.take("shape_constants", [P, K_ALL - K_ROT])
        rot = kshape[:, 0:P]
        ma0 = kshape[:, K_MASK0 - K_ROT:K_MASK - K_ROT]
        mas = kshape[:, K_MASK - K_ROT:K_CAUS - K_ROT]
        mca = kshape[:, K_CAUS - K_ROT:K_COS - K_ROT]
        cos = kshape[:, K_COS - K_ROT:K_SIN - K_ROT]
        sin = kshape[:, K_SIN - K_ROT:K_ALL - K_ROT]
        mo = rr.take("meta_out", [P, NM])
        assert rr.at <= y2_at, rr.at - y2_at
        chi = nc.alloc_sbuf_tensor_at("c_high", [P, CT, L], F32R, offset=big)
        clo = nc.alloc_sbuf_tensor_at("c_low", [P, CT, L], F32R, offset=big + CT * L * 4)
        cgt = nc.alloc_sbuf_tensor_at("c_gate_silu", [P, CT, L], F32, offset=big + 2 * CT * L * 4)
        prow2 = nc.alloc_sbuf_tensor_at("par_rows_layer", [P, 2, P], F32, offset=work2)
        rw = Region(work2)
        pb = rw.take("p_block", [P, 2, 4 * (NM + 2 * BLK) + NM])
        pts = rw.take("p_transposed", [P, 2, 3 * BLK])
        agt = rw.take("a_gate_silu", [P, 2, L])
        ptm = rw.take("p_meta_transposed", [NM, NM])
        cra = rw.take("c_raw", [P, TAPS - 1 + L])
        t1 = rw.take("tmp1", [P, L])
        rx = rw.take("rx_raw", [P, RTAPS + L])
        cacc = rw.take("c_partial", [P, L])
        wa = nc.alloc_sbuf_tensor_at("w_a_diag", [P, P], F32, offset=tri_at)
        wx = rw.take("w_x_diag", [P, P])
        half = (4 * (NM + 2 * BLK) + NM) * 4
        assert 2 * L * 4 <= half
        rcv = nc.alloc_sbuf_tensor_at("r_conv", [P, L], F32, offset=work2)
        rga = nc.alloc_sbuf_tensor_at("r_gate_a", [P, L], F32, offset=work2 + L * 4)
        rgx = nc.alloc_sbuf_tensor_at("r_gate_x", [P, L], F32, offset=work2 + half)
        rth = nc.alloc_sbuf_tensor_at("r_tanh", [P, L], F32, offset=work2 + half + L * 4)
        rgs = t1
        rn = Region(work2 + 2 * P * 4)
        lrb = rn.take("norm_scale_bc", [P, L])
        lsq = rn.take("norm_square", [P, 2, L])
        lt = rn.take("norm_tmp", [P, 2, L])
        tmp2 = lt
        csq = nc.alloc_sbuf_tensor_at("c_square", [P, CT, L], F32, offset=big + 3 * CT * L * 4)
        identr = nc.alloc_sbuf_tensor_at("ident_r", [P, P], F32R, offset=y2_at)
        outn = nc.alloc_sbuf_tensor_at("out_natural", [P, ST, D], F32, offset=big)

        def sem(name):
            return ctx.enter_context(nc.semaphore(name))

        raw_full = [sem(f"raw_full{j}") for j in range(4)]
        hi_ready = sem("hi_ready")
        lo_ready = sem("lo_ready")
        piece_used = sem("piece_used")
        pass0_done = sem("pass0_done")
        evac = sem("evac")
        xh_done = sem("xh_done")
        x_ready = sem("x_ready")
        const_in, par_in, xn_in = sem("const_in"), sem("par_in"), sem("xn_in")
        par_tr, par_ok = sem("par_tr"), sem("par_ok")
        x_ss, x_var, x_sd, xs_ready = sem("x_ss"), sem("x_var"), sem("x_sd"), sem("xs_ready")
        tr_raw, tr_raw_free, tr_sc = sem("tr_raw"), sem("tr_raw_free"), sem("tr_sc")
        x_stored = [sem(f"x_stored{i}") for i in range(4)]
        idr_ok = sem("idr_ok")
        ws_in, ws_masked, wst_tr, wst_ok, rs_mm, rs_ok = (
            sem("ws_in"), sem("ws_masked"), sem("wst_tr"), sem("wst_ok"), sem("rs_mm"), sem("rs_ok"))
        g_z, g_m, g_em, at_tr, at_ok, gr_stored = (
            sem("g_z"), sem("g_m"), sem("g_em"), sem("at_tr"), sem("at_ok"), sem("gr_stored"))
        a_var, a_sd, vn_ready, sgu_done, sv_done, ug_used, yg_done = (
            sem("a_var"), sem("a_sd"), sem("vn_ready"), sem("sgu_done"), sem("sv_done"), sem("ug_used"), sem("yg_done"))
        bc_in, cq_done, qk_ready, s_mm, p_arg, p_exp, p_done = (
            sem("bc_in"), sem("cq_done"), sem("qk_ready"), sem("s_mm"), sem("p_arg"), sem("p_exp"), sem("p_done"))
        pv_m, den_abs, h_ready, sq_ready, ms_mm, rms_rt, zz_used, ym_done = (
            sem("pv_m"), sem("den_abs"), sem("h_ready"), sem("sq_ready"), sem("ms_mm"), sem("rms_rt"),
            sem("zz_used"), sem("ym_done"))
        acc_in, tmp_used, rms_sq, rms_mm, rb_rt, res_done, meta_in, meta_tr, meta_ok = (
            sem("acc_in"), sem("tmp_used"), sem("rms_sq"), sem("rms_mm"), sem("rb_rt"), sem("res_done"),
            sem("meta_in"), sem("meta_tr"), sem("meta_ok"))
        acc_done = sem("acc_done")
        ln_mean, ln_c, ln_sq, ln_mm, ln_rt, ln_t = (
            sem("ln_mean"), sem("ln_c"), sem("ln_sq"), sem("ln_mm"), sem("ln_rt"), sem("ln_t"))
        shape_in, pl_in, pl_tr, pl_ok, sink_in, krd_in = (
            sem("shape_in"), sem("pl_in"), sem("pl_tr"), sem("pl_ok"), sem("sink_in"), sem("krd_in"))
        rot_mm, rope_done, kg_ready, vgr_ready = sem("rot_mm"), sem("rope_done"), sem("kg_ready"), sem("vgr_ready")
        s_done, s_taken, att_max, att_exp, p_ready = (
            sem("s_done"), sem("s_taken"), sem("att_max"), sem("att_exp"), sem("p_ready"))
        pt_done, pt_evac, pv_done, o_taken = sem("pt_done"), sem("pt_evac"), sem("pv_done"), sem("o_taken")
        c_taken, rw_in, r_conved, r_mm, r_act, r_act2, r_w, r_sqrt, lru_done, pads_ok = (
            sem("c_taken"), sem("rw_in"), sem("r_conved"), sem("r_mm"), sem("r_act"), sem("r_act2"), sem("r_w"), sem("r_sqrt"),
            sem("lru_done"), sem("pads_ok"))
        c_gated, c_part, att_sum = sem("c_gated"), sem("c_part"), sem("att_sum")
        lam_exp, sp_ok = sem("lam_exp"), sem("sp_ok")
        cn_mean, cn_c, cn_sq, cn_mm, cn_rt, cn_t, cn_silu, cn_hi, c_ready = (
            sem("cn_mean"), sem("cn_c"), sem("cn_sq"), sem("cn_mm"), sem("cn_rt"), sem("cn_t"), sem("cn_silu"),
            sem("cn_hi"), sem("c_ready"))
        y_conv, res_saved, z_done = sem("y_conv"), sem("res_saved"), sem("z_done")
        fin_mm, fin_ev, out_st = sem("fin_mm"), sem("fin_ev"), sem("out_st")

        halves = lambda b: ps[:, b:b + 2, 0:LH]
        two = lambda t: t.rearrange("p (a n) -> p a n", a=2)
        f = lambda t: t.bitcast(F32)
        plr = lambda c, n: pl[:, c // P, c % P:c % P + n]
        plc = lambda c: pl[:, c // P, c % P:c % P + 1]
        shift = POFF

        block = ctx.enter_context(nc.Block())

        @block.sync
        def _(sp):
            def load(U, src, pair=None, wide=256):
                for j in range(4):
                    if not (isinstance(U, int) and U == 0):
                        sp.wait_ge(lo_ready, 4 * U - 3 + j)
                    for i in range(2):
                        if pair:
                            sp.dma_start(raw[:, j, :, i * P:(i + 1) * P], pair[i](j, slice(0, 4))).then_inc(raw_full[j], 16)
                        else:
                            sp.dma_start(raw[:, j, 2 * i:2 * i + 2, 0:wide], src(j, slice(2 * i, 2 * i + 2))).then_inc(raw_full[j], 16)

            def cols(w, col, n=256, row=0):
                return lambda j, r: w[:, ds(row + 4 * j + r.start, r.stop - r.start), ds(col, n)]

            for i in range(ST):
                sp.dma_start(xn[:, i, :], x_nat[:, i, :]).then_inc(xn_in, 16)
            load(U_GATE, None, (cols(w_in, C_I, P), cols(w_in, C_F, P)))
            with sp.Fori(0, H) as h:
                for n, c in enumerate((C_VG, C_U, C_ZG)):
                    load(U_SGU + 3 * h + n, cols(w_in, c + DV * h))
            with sp.Fori(0, H) as h:
                U = U_MLSTM + 4 * h
                load(U, None, (cols(w_in, C_Q + P * h, P), cols(w_in, C_K + P * h, P)))
                for n, c in enumerate((C_V, C_O, C_Z)):
                    load(U + 1 + n, cols(w_in, c + DV * h))
            with sp.Fori(0, 8) as d:
                load(U_OUT_M + d, cols(w_out, 256 * d))
            with sp.Fori(0, 8) as d:
                load(U_OUT_G + d, cols(w_out, 256 * d, row=KT))
            with sp.Fori(0, LAYERS) as l:
                U = U_LAYER + N_LAYER * l
                load(U + O_K, cols(w_in2, D_K, row=KT * l))
                load(U + O_V, cols(w_in2, D_V, row=KT * l))
                sp.wait_ge(evac, 2 * (U + O_K) + 2)
                for g in range(NKV):
                    for o in (0, HD):
                        s0 = g % 2 * HD
                        sp.dma_start(krd[o:o + HD, g, :], krw[s0:s0 + HD, g // 2, :]).then_inc(krd_in, 16)
                with sp.Fori(0, NKV) as g:
                    V = U + O_GRP + 4 * g
                    load(V, cols(w_in2, D_Q + 256 * g, row=KT * l))
                    load(V + 1, None, (cols(w_in2, D_CV + P * g, P, KT * l), cols(w_in2, D_CG + P * g, P, KT * l)))
                    load(V + 2, cols(w_in2, D_AG + 256 * g, row=KT * l))
                    load(V + 3, None, (cols(w_in2, D_RX + P * g, P, KT * l), cols(w_in2, D_RG + P * g, P, KT * l)))
                with sp.Fori(0, 2) as n:
                    load(U + O_CG + n, cols(w_in2, D_CGATE + 256 * n, row=KT * l))
                load(U + O_PW, lambda j, r: w_pw[:, ds(CT * l + r.start, 2), j * P:(j + 1) * P], wide=P)
                with sp.Fori(0, 8) as d:
                    load(U + O_OUT + d, cols(w_out2, 256 * d, row=KT * l))
            for i in range(ST):
                sp.wait_ge(fin_ev, 4 * i + 4)
                sp.dma_start(out_nat[:, i, :], outn[:, i, :]).then_inc(out_st, 16)
            sp.wait_ge(out_st, 16 * ST)

        @block.gpsimd
        def _(pool):
            for n, c in ((ident, K_IDENT), (ones, K_ONES), (tri, K_TRI)):
                pool.dma_start(n[:], consts[:, c:c + P]).then_inc(const_in, 16)
            row = 0
            for name, n in (("norm_w", 16), ("conv_w", 64), ("conv_b", 16), ("mlstm_norm_w", 16), ("final_norm_w", 16),
                            ("sgu_norm_w", 16), ("sgu_norm_b", 16), ("ln_in_g_2", 16), ("ln_in_b_2", 16)):
                v = a[name]
                v = v.rearrange("j (t p) -> (j t) p", p=P) if len(v.shape) == 2 else v.rearrange("(t p) -> t p", p=P)
                pool.dma_start(prow[row % P:row % P + n, row // P, :], v).then_inc(par_in, 16)
                row += n
            pool.dma_start(small[0:8, 60:61], a["b_igate"].unsqueeze(1)).then_inc(par_in, 16)
            pool.dma_start(small[0:8, 61:62], a["b_fgate"].unsqueeze(1)).then_inc(par_in, 16)
            for d in range(KT):
                pool.wait_ge(tr_raw_free, d + 1)
                pool.dma_start(x_t[:, d, :], stage[:, d % 4, :]).then_inc(x_stored[d % 4], 16)
            pool.wait_ge(x_ready, KT)
            pool.dma_start(ws[:], a["w_spatial"].rearrange("h t s -> t h s")).then_inc(ws_in, 16)
            pool.dma_start(bsp[:], a["b_spatial"].partition_broadcast(P)).then_inc(ws_in, 16)
            pool.wait_ge(ws_in, 32)
            pool.affine_select(out=ws[:], in_=ws[:], compare_op=ALU.is_ge, fill=0.0, base=0,
                               pattern=[[0, H], [-1, P]], channel_multiplier=1).then_inc(ws_masked, 1)
            pool.wait_ge(g_em, 1)
            pool.dma_start(gate_rows, gout[:]).then_inc(gr_stored, 16)
            pool.wait_ge(gr_stored, 16)
            pool.wait_ge(yg_done, H)
            with pool.Fori(0, H) as h:
                pool.wait_ge(h_ready, h)
                pool.dma_start(bc[:], gate_rows[ds(h, 1)].squeeze(0).partition_broadcast(P)).then_inc(bc_in, 16)
            pool.wait_ge(x_ready, 2 * KT)
            for i in range(4):
                pool.wait_ge(x_stored[i], 16 * KT // 4)
            pool.dma_start(acc[:], x_t).then_inc(acc_in, 16)
            pool.dma_start(mnat[:], a["meta_tokens_2"]).then_inc(meta_in, 16)
            pool.wait_ge(pads_ok, 1)
            with pool.Fori(0, LAYERS) as l:
                with pool.Fori(0, NKV) as g:
                    pool.wait_ge(r_mm, 2 * NKV * l + 2 * g)
                    for m, name in ((wa, "lru_wa_2"), (wx, "lru_wx_2")):
                        w = a[name].rearrange("l h i j -> i (l h) j")
                        for o in range(2):
                            pool.dma_start(m[o * HD:(o + 1) * HD, o * HD:(o + 1) * HD].unsqueeze(1),
                                           w[:, ds(8 * l + 2 * g + o, 1), :]).then_inc(rw_in, 16)
                    G = NKV * l + g
                    A = NH * l + GROUP * g
                    W3 = NM + 2 * BLK
                    ct = y2[:, ds(g, 1), :].squeeze(1)

                    def normed(i):
                        pool.drain()
                        pool.wait_ge(att_sum, A + i + 1)
                        pool.tensor_tensor(pb[0:NM, i % 2, 4 * W3:4 * W3 + NM], pb[0:NM, i % 2, 4 * W3:4 * W3 + NM],
                                           small[0:NM, 40:41].broadcast_to([NM, NM]), ALU.mult)
                        p = pb[:, i % 2, 0:NM + BLK]
                        pool.tensor_tensor(p, p, small[:, 36:37].broadcast_to([P, NM + BLK]), ALU.mult)
                        p = pb[:, i % 2, W3:4 * W3].rearrange("p (n w) -> p n w", w=W3)
                        pool.tensor_tensor(p, p, small[:, 37:40].unsqueeze(2).broadcast_to([P, 3, W3]), ALU.mult)\
                            .then_inc(p_ready, 1)

                    def taps(a0, a1):
                        for j in range(a0, a1):
                            wj = pl[:, 0, ds(CT * j + g, 1)].broadcast_to([P, L])
                            if j == 0:
                                ins = pool.tensor_tensor(ct, cra[:, 0:L], wj, ALU.mult)
                            else:
                                pool.drain()
                                pool.tensor_tensor(t1[:], cra[:, j:j + L], wj, ALU.mult)
                                pool.drain()
                                ins = pool.tensor_tensor(ct, ct, t1[:], ALU.add)
                        return ins

                    pool.drain()
                    pool.wait_ge(evac, 2 * (U_LAYER + N_LAYER * l + O_GRP + 4 * g + 1) + 2)
                    pool.tensor_tensor(cra[:, TAPS - 1:], cra[:, TAPS - 1:], agt[:, 0, :], ALU.mult).then_inc(c_gated, 1)
                    normed(0)
                    taps(0, 3)
                    normed(1)
                    taps(3, 6)
                    normed(2)
                    taps(6, PTAPS).then_inc(c_part, 1)
                    normed(3)

        @block.tensor
        def _(pe):
            def three(dst, k, w, tok, m, j, kt, first, last):
                wc = slice(m * P, (m + 1) * P)
                pe.matmul(dst, wh[:, j, kt, wc], xh[:, k, tok], start=first, stop=False)
                pe.matmul(dst, wh[:, j, kt, wc], xl[:, k, tok], start=False, stop=False)
                return pe.matmul(dst, wl[:, j, kt, wc], xh[:, k, tok], start=False, stop=last)

            def three_t(dst, k, tok, j, kt, first, last):
                pe.matmul(dst, xh[:, k, tok], wh[:, j, kt, :], start=first, stop=False)
                pe.matmul(dst, xl[:, k, tok], wh[:, j, kt, :], start=False, stop=False)
                return pe.matmul(dst, xh[:, k, tok], wl[:, j, kt, :], start=False, stop=last)

            def begin(U, m):
                if not (isinstance(U, int) and U == 0):
                    pe.wait_ge(evac, 2 * U + m - 1)

            def end_piece(U, m, j, last):
                if m == 1:
                    last.then_inc(piece_used, 1)
                elif j == 3:
                    last.then_inc(pass0_done, 1)

            def arrive(U, m, j, fill, k=None):
                if m == 0:
                    pe.wait_ge(lo_ready, 4 * U + j + 1)
                    pe.wait_ge(x_ready, fill + 4 * (j + 1))

            def unit(U, fill, wide=False, after=(None, None), mid=(None, None), hook=None):
                for m in range(2):
                    begin(U, m)
                    for j in range(4):
                        arrive(U, m, j, fill)
                        for kt in range(4):
                            k = 4 * j + kt
                            if wide:
                                for q in range(2):
                                    last = three(ps[:, 2 * m + q, 0:LH], k, None, slice(q * LH, (q + 1) * LH), m, j, kt, k == 0, k == KT - 1)
                            else:
                                last = three(ps[:, m, :], k, None, slice(0, S), m, j, kt, k == 0, k == KT - 1)
                        end_piece(U, m, j, last)
                        if j == 1 and mid[m]:
                            mid[m]()
                        if hook:
                            hook(4 * m + j)
                    if after[m]:
                        after[m]()

            def unit_tokens(U, fill, first_token, groups, after=(None, None)):
                for m in range(2):
                    begin(U, m)
                    for i, (dst, tok) in enumerate(groups[m]):
                        for j in range(4):
                            if i == 0:
                                arrive(U, m, j, fill)
                            for kt in range(4):
                                k = 4 * j + kt
                                last = three_t(dst, k, slice(tok, tok + P), j, kt, k == 0, k == KT - 1)
                            if i == len(groups[m]) - 1:
                                end_piece(U, m, j, last)
                    if after[m]:
                        after[m]()

            tok1 = [[(ps[:, m, i * 256:(i + 1) * 256], (2 * m + i) * P) for i in range(2)] for m in range(2)]

            pe.wait_ge(const_in, 48)
            pe.wait_ge(par_in, 16 * 11)
            pe.transpose(ps[:, 0, 0:P], prow[:, 0, :], ident[:])
            pe.transpose(ps[:, 1, 0:ROWS1], prow[0:ROWS1, 1, :], ident[0:ROWS1, 0:ROWS1]).then_inc(par_tr, 1)
            pe.wait_ge(xn_in, 16 * ST)
            for d in range(KT):
                if d >= 4:
                    pe.wait_ge(tr_raw_free, d - 3)
                for i in range(ST):
                    last = pe.transpose(ps[:, 4 + d % 4, i * P:(i + 1) * P], xn[:, i, d * P:(d + 1) * P], ident[:])
                last.then_inc(tr_raw, 1)
            pe.wait_ge(xs_ready, 1)
            for d in range(KT):
                if d < 4:
                    pe.wait_ge(tr_raw_free, KT - 3 + d)
                else:
                    pe.wait_ge(x_ready, d - 3)
                for i in range(ST):
                    last = pe.transpose(ps[:, 4 + d % 4, i * P:(i + 1) * P], xs[:, i, d * P:(d + 1) * P], ident[:])
                last.then_inc(tr_sc, 1)

            unit(U_GATE, 0)
            pe.wait_ge(ws_masked, 1)
            for h in range(H):
                last = pe.transpose(ps[:, 4 + h // 4, h % 4 * P:(h % 4 + 1) * P], ws[:, h, :], ident[:])
            last.then_inc(wst_tr, 1)
            pe.wait_ge(wst_ok, 1)
            for q in range(2):
                last = pe.matmul(ps[:, 6 + q, :], ones[:], wst[:, 4 * q:4 * q + 4, :], start=True, stop=True)
            last.then_inc(rs_mm, 1)
            pe.wait_ge(rs_ok, 1)

            with pe.Fori(0, H) as h:
                U = U_SGU + 3 * h

                def mix():
                    pe.wait_ge(vn_ready, h + 1)
                    pe.wait_ge(sv_done, h)
                    for c in range(2):
                        for n in range(ST):
                            last = pe.matmul(ps[:, 4 + c, n * P:(n + 1) * P], vn[:, n, c * P:(c + 1) * P],
                                             wst[:, ds(h, 1), :], start=True, stop=True)
                    last.then_inc(sgu_done, 1)

                unit_tokens(U, 0, 0, tok1)
                unit(U + 1, 0, after=(mix, None))
                unit(U + 2, 0)

            pe.wait_ge(g_m, 1)
            for i in range(ST):
                last = pe.transpose(ps[:, 6, i * H:(i + 1) * H], gz[0:H, i * P:(i + 1) * P], ident[0:H, 0:H])
            last.then_inc(at_tr, 1)

            with pe.Fori(0, H) as h:
                U = U_MLSTM + 4 * h

                def scores():
                    pe.wait_ge(qk_ready, 2 * h + 2)
                    pe.wait_ge(ym_done, h + 1)
                    pe.wait_ge(at_ok, 1)
                    for j in range(ST):
                        pe.matmul(ps[:, 4 + j, 0:S - j * P], kc[:, j * P:(j + 1) * P], qc[:, j * P:S],
                                  start=True, stop=True).then_inc(s_mm, 1)

                def values():
                    pe.wait_ge(p_done, ST * h + ST)
                    pe.wait_ge(evac, 2 * U + 4)
                    for c in range(3):
                        for j in range(ST):
                            w = vv[:, j, c * P:(c + 1) * P] if c < 2 else ones[:]
                            last = pe.matmul(ps[:, 4 + c, j * P:S], w, pj[:, shift[j]:shift[j] + S - j * P],
                                             start=(j == 0), stop=(j == ST - 1))
                    last.then_inc(pv_m, 1)

                def squares():
                    pe.wait_ge(sq_ready, h + 1)
                    for c in range(2):
                        last = pe.matmul(ps[:, 7, :], ones[:], sq[:, c, :], start=(c == 0), stop=(c == 1))
                    last.then_inc(ms_mm, 1)

                unit(U, 0)
                unit_tokens(U + 1, 0, 0, tok1, after=(scores, None))
                unit(U + 2, 0, after=(values, None))
                unit(U + 3, 0, after=(squares, None))

            with pe.Fori(0, 8) as d:
                unit(U_OUT_M + d, KT)
            with pe.Fori(0, 8) as d:
                unit(U_OUT_G + d, 2 * KT)
            for d in range(KT):
                pe.wait_ge(rms_sq, d + 1)
                pe.matmul(ps[:, 4, :], ones[:], tmp[:, d % 2, :], start=(d == 0), stop=(d == KT - 1)).then_inc(rms_mm, 1)
            pe.wait_ge(meta_in, 16)
            for d in range(KT):
                last = pe.transpose(ps[:, 5, d * NM:(d + 1) * NM], mnat[:, d * P:(d + 1) * P], ident[0:NM, 0:NM])
            last.then_inc(meta_tr, 1)

            def sum_features(src, n, bank, each):
                for d in range(n):
                    if each:
                        pe.wait_ge(each[0], each[1] + d)
                    for q in range(2):
                        last = pe.matmul(ps[:, bank + q, 0:LH], ones[:], src(d)[:, q * LH:(q + 1) * LH],
                                         start=(d == 0), stop=(d == n - 1))
                    if each:
                        last.then_inc(each[2], 1)
                return last

            def norm(n, ready, value):
                pe.wait_ge(ready, value)
                sum_features(lambda d: res[:, d, :], KT, 4, None).then_inc(ln_mean, 1)
                sum_features(lambda d: lsq[:, d % 2, :], KT, 6, (ln_sq, KT * n + 1, ln_mm))

            norm(0, meta_ok, 1)

            with pe.Fori(0, LAYERS) as l:
                U = U_LAYER + N_LAYER * l
                fill = (4 + 2 * l) * KT - KT
                unit(U + O_K, fill, wide=True)
                pe.wait_ge(pl_in, 16 * 12 * (l + 1))
                pe.transpose(ps[:, 4, 0:P], prow2[:, 0, :], ident[:])
                pe.transpose(ps[:, 5, 0:ROWS_L2], prow2[0:ROWS_L2, 1, :], ident[0:ROWS_L2, 0:ROWS_L2]).then_inc(pl_tr, 1)
                unit_tokens(U + O_V, fill, 0, [
                    [(ps[:, i // 2, i % 2 * 256:(i % 2 + 1) * 256], NM + i * P) for i in range(ST)],
                    [(ps[:, 2, 0:256], 0)]])
                with pe.Fori(0, NKV) as g:
                    V = U + O_GRP + 4 * g
                    G = NKV * l + g
                    A = NH * l + GROUP * g

                    def rotate(t):
                        if t == 0:
                            pe.wait_ge(evac, 2 * V + 2)
                            pe.wait_ge(shape_in, 16 * (l + 1))
                            pe.wait_ge(pl_ok, l + 1)
                            pe.wait_ge(krd_in, 128 * (l + 1))
                            pe.wait_ge(r_act, 2 * G)
                            pe.wait_ge(o_taken, 2 * G)
                        if t == 2:
                            pe.wait_ge(rope_done, 3 * G + 1)
                        for q in range(2):
                            rhs = (qrw[:, t, q * LH:(q + 1) * LH] if t < 2
                                   else krd[:, ds(g, 1), q * LH:(q + 1) * LH])
                            last = pe.matmul(ps[:, 4 + 2 * (t % 2) + q, 0:LH], rot, rhs, start=True, stop=True)
                        last.then_inc(rot_mm, 1)

                    def score(i, n):
                        o = i % 2 * HD
                        q = qg[o:o + HD, i // 2, :]
                        bank = 4 + n % 2
                        if n == 0 and i == 0:
                            pe.wait_ge(rope_done, 3 * G + 3)
                        pe.wait_ge(s_taken, 4 * A + 4 * i + n + 1)
                        tq = NM + n * BLK
                        if n < 2:
                            last = pe.matmul(ps[:, bank, 0:NM + (n + 1) * BLK], q[:, tq:tq + BLK],
                                             kg[o:o + HD, 0:NM + (n + 1) * BLK], start=True, stop=True)
                        else:
                            pe.matmul(ps[:, bank, 0:NM], q[:, tq:tq + BLK], kg[o:o + HD, 0:NM], start=True, stop=True)
                            last = pe.matmul(ps[:, bank, NM:NM + 2 * BLK], q[:, tq:tq + BLK],
                                             kg[o:o + HD, tq - BLK:tq + BLK], start=True, stop=True)
                        if n == 0:
                            last = pe.matmul(ps[0:NM, bank, 160:160 + NM], q[:, 0:NM], kg[o:o + HD, 0:NM],
                                             start=True, stop=True)
                        last.then_inc(s_done, 1)

                    def turn(i, n):
                        if n == 0:
                            pe.wait_ge(p_ready, A + i + 1)
                        pe.wait_ge(pt_evac, 4 * A + 4 * i + n)
                        if n == 1:
                            if i == 0:
                                pe.wait_ge(vgr_ready, G + 1)
                            o = i % 2 * HD
                            pe.matmul(ps[o:o + HD, 6, 3 * BLK + 2 * NM:3 * BLK + 3 * NM], vgr[0:NM, 0, :], ptm[:],
                                      start=True, stop=True)
                        c0 = n * (NM + 2 * BLK)
                        pe.transpose(ps[0:NM, 6, 0:BLK], pb[:, i % 2, c0:c0 + NM], ident[:])
                        if n > 0:
                            pe.transpose(ps[:, 6, BLK:2 * BLK], pb[:, i % 2, c0 + NM:c0 + NM + BLK], ident[:])
                            c0 += BLK
                        last = pe.transpose(ps[:, 6, 2 * BLK:3 * BLK], pb[:, i % 2, c0 + NM:c0 + NM + BLK], ident[:])
                        if n == 0:
                            cm = 4 * (NM + 2 * BLK)
                            last = pe.transpose(ps[0:NM, 6, 3 * BLK:3 * BLK + NM], pb[0:NM, i % 2, cm:cm + NM],
                                                ident[0:NM, 0:NM])
                        last.then_inc(pt_done, 1)

                    def value(i, n):
                        o = i % 2 * HD
                        if n == 0 and i % 2 == 0:
                            pe.wait_ge(o_taken, 2 * G + i // 2)
                        pe.wait_ge(pt_evac, 4 * A + 4 * i + n + 1)
                        dst = ps[o:o + HD, 7, n * BLK:(n + 1) * BLK]
                        pe.matmul(dst, vgr[0:NM, 0, :], pts[0:NM, n % 2, 0:BLK], start=True, stop=False)
                        if n > 0:
                            pe.matmul(dst, vgr[:, n, :], pts[:, n % 2, BLK:2 * BLK], start=False, stop=False)
                        last = pe.matmul(dst, vgr[:, n + 1, :], pts[:, n % 2, 2 * BLK:3 * BLK], start=False, stop=True)
                        if n == 3:
                            last.then_inc(pv_done, 1)

                    def step(k):
                        if k < 4 * GROUP:
                            score(k // 4, k % 4)
                        if 7 <= k < 7 + 4 * GROUP:
                            value((k - 7) // 4, (k - 7) % 4)
                        if 6 <= k < 6 + 4 * GROUP:
                            turn((k - 6) // 4, (k - 6) % 4)

                    def recur(t):
                        if t == 0:
                            pe.wait_ge(r_conved, G + 1)
                            pe.wait_ge(rw_in, 64 * (G + 1))
                            pe.wait_ge(s_taken, 4 * A + 18)
                        else:
                            pe.wait_ge(r_act, 2 * G + 1)
                        for q in range(2):
                            last = pe.matmul(ps[:, 4 + q, 0:LH], (wa, wx)[t][:], rcv[:, q * LH:(q + 1) * LH],
                                             start=True, stop=True)
                        last.then_inc(r_mm, 1)

                    def behind(first):
                        def hook(n):
                            n += first
                            if n == 8:
                                rotate(0)
                                rotate(1)
                            elif n == 9:
                                rotate(2)
                            elif n >= 11:
                                step(n - 11)
                        return hook

                    unit(V, fill, wide=True)
                    unit(V + 1, fill, wide=True, hook=behind(8))
                    unit(V + 2, fill, wide=True, hook=behind(16))
                    unit(V + 3, fill, wide=True, hook=behind(24))
                    recur(0)
                    step(21)
                    step(22)
                    recur(1)

                def c_mean():
                    pe.wait_ge(lru_done, NKV * (l + 1))
                    pe.wait_ge(c_taken, NKV * (l + 1))
                    sum_features(lambda d: y2[:, d, :], CT, 4, None).then_inc(cn_mean, 1)

                def c_var():
                    pe.wait_ge(cn_sq, CT * (l + 1))
                    sum_features(lambda d: csq[:, d, :], CT, 6, None).then_inc(cn_mm, 1)

                unit(U + O_CG, fill, wide=True, after=(c_mean, None), mid=(None, c_var))
                unit(U + O_CG + 1, fill, wide=True)
                pe.wait_ge(c_ready, CT * (l + 1))
                pe.wait_ge(cn_rt, l + 1)
                pe.wait_ge(evac, 2 * (U + O_PW))
                for t in range(CT):
                    pe.wait_ge(lo_ready, 4 * (U + O_PW) + t + 1)
                    for k in range(CT):
                        for q in range(2):
                            tok = slice(q * LH, (q + 1) * LH)
                            dst = ps[:, 2 * t + q, 0:LH]
                            first = pe.matmul(dst, wh[:, t, k, 0:P], chi[:, k, tok], start=(k == 0), stop=False)
                            if t == k == q == 0:
                                first.then_inc(pass0_done, 1)
                            pe.matmul(dst, wh[:, t, k, 0:P], clo[:, k, tok], start=False, stop=False)
                            last = pe.matmul(dst, wl[:, t, k, 0:P], chi[:, k, tok], start=False, stop=(k == CT - 1))
                    last.then_inc(piece_used, 1)
                with pe.Fori(0, 8) as d:
                    unit(U + O_OUT + d, fill + KT, wide=True)
                norm(l + 1, z_done, KT * (l + 1))

            pe.wait_ge(idr_ok, 1)
            pe.wait_ge(x_ready, (4 + 2 * LAYERS) * KT)
            for i in range(ST):
                for q in range(4):
                    n = 4 * i + q
                    if n >= 8:
                        pe.wait_ge(fin_ev, n - 7)
                    for e in range(4):
                        dst = ps[:, n % 8, e * P:(e + 1) * P]
                        tok = slice(NM + i * P, NM + (i + 1) * P)
                        pe.matmul(dst, xh[:, 4 * q + e, tok], identr[:], start=True, stop=False)
                        last = pe.matmul(dst, xl[:, 4 * q + e, tok], identr[:], start=False, stop=True)
                    last.then_inc(fin_mm, 1)

        @block.scalar
        def _(act):
            def high(U, j):
                act.wait_ge(raw_full[j], 32 * U + 32)
                if not (isinstance(U, int) and U == 0):
                    act.wait_ge(piece_used, 4 * U - 3 + j)
                act.activation(wh[:, j], raw[:, j], ACT.Copy).then_inc(hi_ready, 1)

            def passed(U, m):
                if m == 0:
                    act.wait_ge(pass0_done, U + 1)
                else:
                    act.wait_ge(piece_used, 4 * U + 4)

            def take(U, m, dst, src, fn=ACT.Copy, **kw):
                passed(U, m)
                act.activation(dst, src, fn, **kw).then_inc(evac, 1)

            act.wait_ge(xn_in, 16 * ST)
            for i in range(ST):
                act.activation(xs[:, i, :], xn[:, i, :], ACT.Square, accum_out=small[:, i:i + 1])
                act.drain()
            act.sem_inc(x_ss, 1)
            for j in range(4):
                high(0, j)
            act.wait_ge(par_tr, 1)
            act.activation(par[:, 0, :], ps[:, 0, 0:P], ACT.Copy)
            act.activation(par[:, 1, 0:ROWS1], ps[:, 1, 0:ROWS1], ACT.Copy).then_inc(par_ok, 1)
            act.wait_ge(x_var, 1)
            act.activation(small[:, 8:12], small[:, 4:8], ACT.Sqrt).then_inc(x_sd, 1)
            for d in range(KT):
                act.wait_ge(tr_raw, d + 1)
                if d >= 4:
                    act.wait_ge(x_stored[d % 4], 16 * (d // 4))
                act.activation(stage[:, d % 4, :], ps[:, 4 + d % 4, :], ACT.Copy).then_inc(tr_raw_free, 1)
            act.drain()
            for d in range(KT):
                act.wait_ge(tr_sc, d + 1)
                act.activation(xh[:, d, 0:S], ps[:, 4 + d % 4, :], ACT.Copy, scale=par[:, 0, PR_NORM + d:PR_NORM + d + 1])\
                   .then_inc(xh_done, 1)

            take(0, 0, li[:], ps[0:H, 0, :], ACT.Identity, bias=small[0:H, 60:61])
            for j in range(4):
                high(1, j)
            take(0, 1, xf[:], ps[0:H, 1, :], ACT.Identity, bias=small[0:H, 61:62])
            act.drain()
            act.activation(gz[:], xf[:], ACT.Abs)
            act.drain()
            act.activation(gz[:], gz[:], ACT.Exp, scale=-1.0).then_inc(g_z, 1)
            act.wait_ge(wst_tr, 1)
            act.activation(wst[:].rearrange("p h t -> p (h t)"), ps[:, 4:6, :].rearrange("p a n -> p (a n)"), ACT.Copy)\
               .then_inc(wst_ok, 1)
            act.wait_ge(rs_mm, 1)
            act.activation(rsb[:].rearrange("p h t -> p (h t)"), ps[:, 6:8, :].rearrange("p a n -> p (a n)"), ACT.Copy)\
               .then_inc(rs_ok, 1)
            act.wait_ge(g_m, 1)
            act.activation(gout[:, 1, :], gq[:], ACT.Exp, scale=-1.0).then_inc(g_em, 1)

            with act.Fori(0, H) as h:
                U = U_SGU + 3 * h
                act.wait_ge(vn_ready, h)
                for m in range(2):
                    take(U, m, vg[:, 2 * m:2 * m + 2, :], ps[:, m, :].rearrange("p (a n) -> p a n", a=2), ACT.Gelu_apprx_tanh)
                    if m == 0:
                        for j in range(4):
                            high(U + 1, j)
                act.wait_ge(a_var, h + 1)
                act.activation(small[:, 52:56], small[:, 48:52], ACT.Sqrt).then_inc(a_sd, 1)
                act.wait_ge(ug_used, h)
                for m in range(2):
                    take(U + 1, m, ug[:, m, :], ps[:, m, :], ACT.Gelu_apprx_tanh)
                    if m == 0:
                        for j in range(4):
                            high(U + 2, j)
                act.wait_ge(yg_done, h)
                for m in range(2):
                    take(U + 2, m, zg[:, m, :], ps[:, m, :], ACT.Silu)
                    if m == 0:
                        for j in range(4):
                            high(U + 3, j)

            act.wait_ge(at_tr, 1)
            act.activation(at[:].rearrange("p i h -> p (i h)"), ps[:, 6, 0:ST * H], ACT.Copy).then_inc(at_ok, 1)
            act.wait_ge(yg_done, H)
            act.drain()

            with act.Fori(0, H) as h:
                U = U_MLSTM + 4 * h

                def silu(t, n, col):
                    act.wait_ge(cq_done, 2 * h + n)
                    act.activation(t[:], t[:], ACT.Silu, bias=par[:, 0, ds(col + h, 1)]).then_inc(qk_ready, 1)

                act.wait_ge(ym_done, h + 1)
                take(U, 0, cr[:, 3:3 + S], ps[:, 0, :])
                silu(qc, 1, PR_CONVB)
                for j in range(4):
                    high(U + 1, j)
                take(U, 1, cr[:, 3:3 + S], ps[:, 1, :])
                silu(kc, 2, PR_CONVB + H)
                act.wait_ge(pv_m, h)
                take(U + 1, 0, vv[:, 0:2, :], ps[:, 0, :].rearrange("p (a n) -> p a n", a=2))
                for j in range(ST):
                    act.wait_ge(p_arg, ST * h + j + 1)
                    pjj = pj[:, shift[j]:shift[j] + S - j * P]
                    act.activation(pjj, pjj, ACT.Exp).then_inc(p_exp, 1)
                for j in range(4):
                    high(U + 2, j)
                take(U + 1, 1, vv[:, 2:4, :], ps[:, 1, :].rearrange("p (a n) -> p a n", a=2))
                take(U + 2, 0, og[:, 0, :], ps[:, 0, :], ACT.Sigmoid)
                high(U + 3, 0)
                act.wait_ge(pv_m, h + 1)
                act.activation(rd[:], ps[:, 6, :], ACT.Abs).then_inc(den_abs, 1)
                for j in range(1, 4):
                    high(U + 3, j)
                act.wait_ge(h_ready, h + 1)
                act.activation(sq[:], ym[:, ds(2 * h, 2), :], ACT.Square).then_inc(sq_ready, 1)
                take(U + 2, 1, og[:, 1, :], ps[:, 1, :], ACT.Sigmoid)
                act.wait_ge(zz_used, 2 * h)
                take(U + 3, 0, zz[:], ps[:, 0, :], ACT.Silu)
                act.wait_ge(ms_mm, h + 1)
                act.activation(rd[:], ps[:, 7, :], ACT.Sqrt, scale=1.0 / DV, bias=small[:, 62:63]).then_inc(rms_rt, 1)
                for j in range(4):
                    high(U + 4, j)
                act.wait_ge(zz_used, 2 * h + 1)
                take(U + 3, 1, zz[:], ps[:, 1, :], ACT.Silu)

            def fill(src, wide, U, start=0):
                act.wait_ge(piece_used, 4 * U)
                with act.Fori(0, KT) as k:
                    act.activation(xh[:, ds(k, 1), 0:wide], src[:, ds(k, 1), 0:wide], ACT.Copy).then_inc(xh_done, 1)

            act.wait_ge(ym_done, H + 1)
            fill(ym, S, U_OUT_M)
            for half_, U0 in ((0, U_OUT_M), (1, U_OUT_G)):
                if half_:
                    fill(yg, S, U_OUT_G)
                def out_unit(d, more):
                    for m in range(2):
                        act.wait_ge(tmp_used, 16 * half_ + 2 * d + m + 1)
                        take(U0 + d, m, tmp[:, m, :], ps[:, m, :])
                        if m == 0 and more:
                            for j in range(4):
                                high(U0 + d + 1, j)
                with act.Fori(0, 8 if not half_ else 7) as d:
                    out_unit(d, True)
                if half_:
                    out_unit(7, False)
            act.wait_ge(acc_done, 2 * KT)
            act.drain()
            for d in range(KT):
                if d >= 2:
                    act.wait_ge(rms_mm, d - 1)
                act.activation(tmp[:, d % 2, :], acc[:, d, :], ACT.Square).then_inc(rms_sq, 1)
            act.wait_ge(rms_mm, KT)
            act.activation(rb1[:], ps[:, 4, :], ACT.Sqrt, scale=1.0 / D, bias=small[:, 62:63]).then_inc(rb_rt, 1)
            act.wait_ge(meta_tr, 1)
            act.wait_ge(res_done, 1)
            act.activation(res[:, :, 0:NM], ps[:, 5, 0:KT * NM].rearrange("p (d n) -> p d n", n=NM), ACT.Copy).then_inc(meta_ok, 1)

            def norm(n, b):
                for d in range(KT):
                    act.wait_ge(ln_c, KT * n + d + 1)
                    if d >= 2:
                        act.wait_ge(ln_mm, KT * n + d - 1)
                    act.activation(lsq[:, d % 2, :], res[:, d, :], ACT.Square).then_inc(ln_sq, 1)
                act.wait_ge(ln_mm, KT * n + KT)
                act.activation(two(lrb[:]), halves(6), ACT.Sqrt, scale=1.0 / D, bias=small[:, 63:64]).then_inc(ln_rt, 1)
                for d in range(KT):
                    act.wait_ge(ln_t, KT * n + d + 1)
                    act.activation(xh[:, d, :], lt[:, d % 2, :], ACT.Identity, bias=b(d)).then_inc(xh_done, 1)

            act.wait_ge(piece_used, 4 * U_LAYER)
            norm(0, lambda d: par[:, 1, PR_LNB - P + d:PR_LNB - P + d + 1])

            with act.Fori(0, LAYERS) as l:
                U = U_LAYER + N_LAYER * l
                for j in range(4):
                    high(U, j)
                act.wait_ge(x_ready, 4 * KT + 2 * KT * l)
                act.dma_start(kshape[:], consts[:, K_ROT:K_ALL]).then_inc(shape_in, 16)
                row = 0
                for name, n in (("conv_dw_w_2", TAPS * CT), ("conv_dw_b_2", CT), ("conv_ln_g_2", CT), ("conv_ln_b_2", CT),
                                ("conv_pw_b_2", CT), ("lru_conv_w_2", RTAPS * CT), ("lru_conv_b_2", CT), ("lru_ba_2", CT),
                                ("lru_bx_2", CT), ("lru_lambda_2", CT), ("ln_post_g_2", KT), ("ln_post_b_2", KT)):
                    v = a[name]
                    v = (v.rearrange("l j (t p) -> l (j t) p", p=P) if len(v.shape) == 3
                         else v.rearrange("l (t p) -> l t p", p=P))
                    act.dma_start(prow2[row % P:row % P + n, row // P, :], v[ds(l, 1)].squeeze(0)).then_inc(pl_in, 16)
                    row += n
                act.dma_start(small[:, 0:NH], a["attn_sinks_2"][ds(l, 1)].squeeze(0).partition_broadcast(P)).then_inc(sink_in, 16)
                for m in range(2):
                    take(U + O_K, m, two(krw[:, m, :]), halves(2 * m))
                    if m == 0:
                        for j in range(4):
                            high(U + O_V, j)
                act.wait_ge(pl_tr, l + 1)
                act.activation(pl[:, 0, :], ps[:, 4, 0:P], ACT.Copy)
                act.activation(pl[:, 1, 0:ROWS_L2], ps[:, 5, 0:ROWS_L2], ACT.Copy).then_inc(pl_ok, 1)
                act.drain()
                act.activation(small[:, 41:45], plr(PL_LAM, CT), ACT.Abs)
                act.drain()
                act.activation(small[:, 41:45], small[:, 41:45], ACT.Exp, scale=-1.0).then_inc(lam_exp, 1)
                take(U + O_V, 0, v2[:, 1:1 + ST, :], ps[:, 0:2, :].rearrange("p a (b n) -> p (a b) n", b=2))
                for j in range(4):
                    high(U + O_V + 1, j)
                take(U + O_V, 1, v2[:, 0, :], ps[:, 2, 0:256])
                act.drain()
                act.wait_ge(krd_in, 128 * (l + 1))
                act.wait_ge(pads_ok, 1)

                with act.Fori(0, NKV) as g:
                    V = U + O_GRP + 4 * g
                    G = NKV * l + g
                    A = NH * l + GROUP * g

                    def exps(i):
                        act.wait_ge(att_max, A + i + 1)
                        w = NM + 2 * BLK
                        for n in range(ST):
                            p = pb[:, i % 2, n * w:n * w + (w if n else NM + BLK)]
                            act.activation(p, p, ACT.Exp, bias=small[:, 21 + n:22 + n], accum_out=small[:, 26 + n:27 + n])
                        p = pb[0:NM, i % 2, 4 * w:4 * w + NM]
                        act.activation(p, p, ACT.Exp, bias=small[0:NM, 25:26], accum_out=small[0:NM, 30:31])
                        act.activation(small[:, 31:36], small[:, 21:26], ACT.Exp,
                                       bias=small[:, ds(GROUP * g + i, 1)]).then_inc(att_exp, 1)

                    def turned(i, n):
                        act.wait_ge(pt_done, 4 * A + 4 * i + n + 1)
                        if n == 0:
                            act.activation(ptm[:], ps[0:NM, 6, 3 * BLK:3 * BLK + NM], ACT.Copy)
                        if n == 1 and i % 2:
                            act.wait_ge(o_taken, 2 * G + i // 2)
                            act.activation(mo[:], ps[:, 6, 3 * BLK + 2 * NM:3 * BLK + 3 * NM], ACT.Copy)
                        act.activation(pts[:, n % 2, :], ps[:, 6, 0:3 * BLK], ACT.Copy).then_inc(pt_evac, 1)

                    def gate(t, dst, b):
                        act.wait_ge(r_mm, 2 * G + t + 1)
                        act.activation(two(dst[:]), halves(4), ACT.Sigmoid, bias=pl[:, 1, ds(b - P + g, 1)]).then_inc(r_act, 1)

                    act.wait_ge(rope_done, 3 * G)
                    take(V, 0, two(qrw[:, 0, :]), halves(0))
                    high(V + 1, 0)
                    high(V + 1, 1)
                    high(V + 1, 2)
                    take(V, 1, two(qrw[:, 1, :]), halves(2))
                    high(V + 1, 3)
                    act.wait_ge(pv_done, A)
                    act.activation(vgr[:], v2[:, :, ds(HD * g, HD)], ACT.Copy).then_inc(vgr_ready, 1)
                    act.wait_ge(c_taken, G)
                    take(V + 1, 0, two(cra[:, TAPS - 1:]), halves(0))
                    high(V + 2, 0)
                    high(V + 2, 1)
                    high(V + 2, 2)
                    exps(0)
                    act.wait_ge(o_taken, 2 * G)
                    take(V + 1, 1, two(agt[:, 0, :]), halves(2), ACT.Sigmoid)
                    high(V + 2, 3)
                    turned(0, 0)
                    turned(0, 1)
                    exps(1)
                    turned(0, 2)
                    act.wait_ge(c_gated, G + 1)
                    take(V + 2, 0, two(agt[:, 0, :]), halves(0), ACT.Silu)
                    turned(0, 3)
                    high(V + 3, 0)
                    turned(1, 0)
                    high(V + 3, 1)
                    turned(1, 1)
                    high(V + 3, 2)
                    exps(2)
                    turned(1, 2)
                    take(V + 2, 1, two(agt[:, 1, :]), halves(2), ACT.Silu)
                    high(V + 3, 3)
                    turned(1, 3)
                    turned(2, 0)
                    turned(2, 1)
                    exps(3)
                    turned(2, 2)
                    take(V + 3, 0, two(rx[:, RTAPS - 1:RTAPS - 1 + L]), halves(0))
                    turned(2, 3)
                    high(V + 4, 0)
                    turned(3, 0)
                    high(V + 4, 1)
                    turned(3, 1)
                    high(V + 4, 2)
                    turned(3, 2)
                    gate(0, rga, PL_BA)
                    turned(3, 3)
                    high(V + 4, 3)
                    gate(1, rgx, PL_BX)
                    act.wait_ge(c_part, G + 1)
                    take(V + 3, 1, two(rgs[:]), halves(2), ACT.Silu)
                    act.drain()
                    act.activation(rth[:], rga[:], ACT.Tanh, scale=small[:, ds(49 + g, 1)])
                    act.drain()
                    act.activation(rga[:], rga[:], ACT.Exp, scale=small[:, ds(45 + g, 1)]).then_inc(r_act2, 1)
                    act.wait_ge(r_w, G + 1)
                    act.activation(rth[:], rth[:], ACT.Sqrt).then_inc(r_sqrt, 1)

                act.wait_ge(lru_done, NKV * (l + 1))
                C = U + O_CG
                take(C, 0, two(cgt[:, 0, :]), halves(0), ACT.Silu)
                for d in range(CT):
                    act.wait_ge(cn_c, CT * l + d + 1)
                    act.activation(csq[:, d, :], y2[:, d, :], ACT.Square).then_inc(cn_sq, 1)
                for j in range(4):
                    high(C + 1, j)
                take(C, 1, two(cgt[:, 1, :]), halves(2), ACT.Silu)
                act.wait_ge(cn_mm, l + 1)
                act.activation(two(lrb[:]), halves(6), ACT.Sqrt, scale=1.0 / CW, bias=small[:, 63:64]).then_inc(cn_rt, 1)
                for d in range(CT):
                    act.wait_ge(cn_t, CT * l + d + 1)
                    act.activation(y2[:, d, :], y2[:, d, :], ACT.Silu, bias=pl[:, 1, PL_CLB - P + d:PL_CLB - P + d + 1])
                    act.drain()
                    act.activation(chi[:, d, :], y2[:, d, :], ACT.Copy).then_inc(cn_hi, 1)
                take(C + 1, 0, two(cgt[:, 2, :]), halves(0), ACT.Silu)
                for j in range(4):
                    high(C + 2, j)
                take(C + 1, 1, two(cgt[:, 3, :]), halves(2), ACT.Silu)
                act.wait_ge(c_ready, CT * (l + 1))
                W = U + O_PW
                for t in range(CT):
                    act.wait_ge(piece_used, 4 * W + t + 1)
                    ins = act.activation(two(y2[:, t, :]), halves(2 * t), ACT.Identity, bias=pl[:, 1, PL_PWB - P + t:PL_PWB - P + t + 1])
                    if t % 2:
                        ins.then_inc(evac, 1)
                for j in range(4):
                    high(W + 1, j)
                act.wait_ge(y_conv, l + 1)
                with act.Fori(0, KT) as k:
                    act.wait_ge(res_saved, KT * l + k + 1)
                    act.activation(xh[:, ds(k, 1), :], y2[:, ds(k, 1), :], ACT.Copy).then_inc(xh_done, 1)

                def out_unit(d, more):
                    for m in range(2):
                        act.wait_ge(tmp_used, 32 + KT * l + 2 * d + m + 1)
                        take(U + O_OUT + d, m, two(tmp2[:, m, :]), halves(2 * m))
                        if m == 0 and more:
                            for j in range(4):
                                high(U + O_OUT + d + 1, j)
                with act.Fori(0, 7) as d:
                    out_unit(d, True)
                out_unit(7, False)
                norm(l + 1, lambda d: plc(PL_PB + d))

            act.activation(identr[:], ident[:], ACT.Copy).then_inc(idr_ok, 1)
            for n in range(KT):
                act.wait_ge(fin_mm, n + 1)
                act.activation(outn[:, n // 4, n % 4 * 512:(n % 4 + 1) * 512], ps[:, n % 8, :], ACT.Copy).then_inc(fin_ev, 1)

        @block.vector
        def _(dve):
            def low(U, j):
                dve.wait_ge(hi_ready, 4 * U + j + 1)
                dve.tensor_tensor(wl[:, j], raw[:, j], f(wh[:, j]), ALU.subtract).then_inc(lo_ready, 1)

            def lows(U, js=range(4)):
                for j in js:
                    low(U, j)

            def log1p(w, q, p, z):
                dve.tensor_scalar(w, z, 2.0, None, ALU.add)
                dve.drain()
                dve.reciprocal(w, w)
                dve.drain()
                dve.tensor_tensor(w, w, z, ALU.mult)
                dve.drain()
                dve.tensor_tensor(q, w, w, ALU.mult)
                dve.drain()
                dve.tensor_scalar(p, q, LOG1P[8], None, ALU.mult)
                dve.drain()
                for c in LOG1P[7:0:-1]:
                    dve.scalar_tensor_tensor(p, p, c, q, ALU.add, ALU.mult)
                    dve.drain()
                dve.scalar_tensor_tensor(p, p, LOG1P[0], w, ALU.add, ALU.mult)
                dve.drain()

            dve.memset(small[:, 62:63], EPS)
            dve.memset(small[:, 63:64], LN_EPS)
            dve.wait_ge(x_ss, 1)
            dve.tensor_scalar(small[:, 4:8], small[:, 0:4], 1.0 / D, EPS, ALU.mult, ALU.add).then_inc(x_var, 1)
            dve.wait_ge(x_sd, 1)
            dve.reciprocal(small[:, 12:16], small[:, 8:12])
            dve.drain()
            for i in range(ST):
                last = dve.tensor_scalar(xs[:, i, :], xn[:, i, :], small[:, 12 + i:13 + i], None, ALU.mult)
            last.then_inc(xs_ready, 1)
            lows(0)
            dve.wait_ge(par_ok, 1)
            for d in range(KT):
                dve.wait_ge(xh_done, d + 1)
                dve.scalar_tensor_tensor(xl[:, d, 0:S], ps[:, 4 + d % 4, :], par[:, 0, PR_NORM + d:PR_NORM + d + 1],
                                         f(xh[:, d, 0:S]), ALU.mult, ALU.subtract).then_inc(x_ready, 1)
            lows(1)
            dve.wait_ge(g_z, 1)
            log1p(gw[:], gq[:], gp[:], gz[:])
            dve.tensor_scalar(gz[:], gp[:], -2.0, None, ALU.mult)
            dve.memset(gq[:], 0.0)
            dve.drain()
            dve.scalar_tensor_tensor(gz[:], xf[:], 0.0, gz[:], ALU.min, ALU.add)
            dve.drain()
            dve.tensor_tensor_scan(gw[:], gz[:], gq[:], 0.0, ALU.add, ALU.add)
            dve.drain()
            dve.tensor_tensor(gz[:], li[:], gw[:], ALU.subtract)
            dve.drain()
            dve.tensor_tensor_scan(gp[:], gz[:], gz[:], 0.0, ALU.max, ALU.max)
            dve.drain()
            dve.tensor_scalar(gout[:, 0, :], gp[:], -1.0, None, ALU.mult)
            dve.tensor_tensor(gq[:], gw[:], gp[:], ALU.add).then_inc(g_m, 1)
            dve.wait_ge(rs_ok, 1)
            dve.wait_ge(ws_in, 32)

            with dve.Fori(0, H) as h:
                U = U_SGU + 3 * h
                lows(U + 1)
                dve.wait_ge(evac, 2 * U + 2)
                for i in range(ST):
                    dve.bn_stats(small[:, 16 + 6 * i:22 + 6 * i], vg[:, i, :])
                dve.drain()
                for i in range(ST):
                    dve.bn_aggr(small[:, 40 + 2 * i:42 + 2 * i], small[:, 16 + 6 * i:22 + 6 * i])
                dve.drain()
                dve.tensor_scalar(small[:, 48:52].unsqueeze(2), small[:, 40:48].rearrange("p (i t) -> p i t", t=2)[:, :, 1:2], EPS, None, ALU.add)\
                   .then_inc(a_var, 1)
                dve.wait_ge(a_sd, h + 1)
                dve.reciprocal(small[:, 56:60], small[:, 52:56])
                dve.drain()
                for i in range(ST):
                    last = dve.tensor_scalar(vn[:, i, :], vg[:, i, :], small[:, 40 + 2 * i:41 + 2 * i],
                                             small[:, 56 + i:57 + i], ALU.subtract, ALU.mult)
                last.then_inc(vn_ready, 1)
                for c in range(2):
                    dve.scalar_tensor_tensor(svr[:, c, :], rsb[:, ds(h, 1), :].squeeze(1), par[:, 1, ds(PR_SGUB - P + 2 * h + c, 1)],
                                             bsp[:, ds(h, 1), :].squeeze(1), ALU.mult, ALU.add)
                dve.drain()
                dve.wait_ge(sgu_done, h + 1)
                for c in range(2):
                    last = dve.scalar_tensor_tensor(sv[:, c, :].rearrange("p (n t) -> p n t", t=P),
                                                    ps[:, 4 + c, :].rearrange("p (n t) -> p n t", t=P),
                                                    par[:, 1, ds(PR_SGUW - P + 2 * h + c, 1)],
                                                    svr[:, c:c + 1, :].broadcast_to([P, ST, P]), ALU.mult, ALU.add)
                last.then_inc(sv_done, 1)
                lows(U + 2)
                dve.drain()
                dve.wait_ge(evac, 2 * (U + 1) + 2)
                dve.tensor_tensor(sv[:], sv[:], ug[:], ALU.mult).then_inc(ug_used, 1)
                lows(U + 3)
                dve.drain()
                dve.wait_ge(evac, 2 * (U + 2) + 2)
                dve.tensor_tensor(yg[:, ds(2 * h, 2), :], sv[:], zg[:], ALU.mult).then_inc(yg_done, 1)

            dve.drain()
            dve.memset(cr[:, 0:3], 0.0).then_inc(ym_done, 1)

            with dve.Fori(0, H) as h:
                U = U_MLSTM + 4 * h

                def conv(dst, col):
                    dve.tensor_scalar(dst[:], cr[:, 0:S], par[:, 0, ds(PR_CONVW + col + h, 1)], None, ALU.mult)
                    dve.drain()
                    for j in range(1, 4):
                        ins = dve.scalar_tensor_tensor(dst[:], cr[:, j:j + S], par[:, 0, ds(PR_CONVW + 16 * j + col + h, 1)],
                                                       dst[:], ALU.mult, ALU.add)
                        if j < 3:
                            dve.drain()
                    ins.then_inc(cq_done, 1)

                dve.wait_ge(evac, 2 * U + 1)
                dve.wait_ge(s_mm, ST * h)
                conv(qc, 0)
                lows(U + 1)
                dve.wait_ge(evac, 2 * U + 2)
                conv(kc, H)
                dve.wait_ge(bc_in, 16 * h + 16)
                dve.wait_ge(at_ok, 1)
                dve.wait_ge(ms_mm, h)
                for j in range(ST):
                    dve.tensor_scalar(pj[:, shift[j]:shift[j] + S - j * P], bc[:, 0, j * P:S], at[:, j, ds(h, 1)], 0.0,
                                      ALU.add, ALU.min).then_inc(p_arg, 1)
                for j in range(ST):
                    dve.wait_ge(p_exp, ST * h + j + 1)
                    dve.wait_ge(s_mm, ST * h + j + 1)
                    pjj = pj[:, shift[j]:shift[j] + S - j * P]
                    dve.scalar_tensor_tensor(pjj, ps[:, 4 + j, 0:S - j * P], float(P) ** -0.5, pjj, ALU.mult, ALU.mult)
                    dve.drain()
                    dve.tensor_tensor(pjj[:, 0:P], pjj[:, 0:P], tri[:], ALU.mult).then_inc(p_done, 1)
                lows(U + 2)
                low(U + 3, 0)
                dve.wait_ge(den_abs, h + 1)
                dve.tensor_tensor(rd[:], rd[:], bc[:, 1, :], ALU.max)
                dve.drain()
                dve.reciprocal(rd[:], rd[:])
                dve.drain()
                last = dve.tensor_tensor(ym[:, ds(2 * h, 2), :], ps[:, 4:6, :], rd[:].unsqueeze(1).broadcast_to([P, 2, S]), ALU.mult)
                last.then_inc(h_ready, 1)
                lows(U + 3, range(1, 4))
                dve.wait_ge(evac, 2 * (U + 3) + 1)
                dve.tensor_tensor(og[:, 0, :], og[:, 0, :], zz[:], ALU.mult).then_inc(zz_used, 1)
                dve.wait_ge(rms_rt, h + 1)
                dve.reciprocal(rd[:], rd[:])
                dve.drain()
                dve.tensor_tensor(ym[:, ds(2 * h, 2), :], ym[:, ds(2 * h, 2), :], rd[:].unsqueeze(1).broadcast_to([P, 2, S]), ALU.mult)
                lows(U + 4)
                dve.wait_ge(evac, 2 * (U + 3) + 2)
                dve.tensor_tensor(og[:, 1, :], og[:, 1, :], zz[:], ALU.mult).then_inc(zz_used, 1)
                dve.drain()
                dve.memset(cr[:, 0:3], 0.0)
                dve.drain()
                for c in range(2):
                    y = ym[:, ds(2 * h + c, 1), :].squeeze(1)
                    last = dve.scalar_tensor_tensor(y, y, par[:, 0, ds(PR_MNORM + 2 * h + c, 1)], og[:, c, :], ALU.mult, ALU.mult)
                last.then_inc(ym_done, 1)

            def fill(src, wide, base):
                with dve.Fori(0, KT) as k:
                    dve.wait_ge(xh_done, base + k + 1)
                    dve.tensor_tensor(xl[:, ds(k, 1), 0:wide], src[:, ds(k, 1), 0:wide], f(xh[:, ds(k, 1), 0:wide]), ALU.subtract)\
                       .then_inc(x_ready, 1)

            dve.drain()
            dve.memset(sqs[:, 0:1], 0.0).then_inc(tmp_used, 2)
            fill(ym, S, KT)
            for half_, U0 in ((0, U_OUT_M), (1, U_OUT_G)):
                if half_:
                    fill(yg, S, 2 * KT)
                def out_unit(d, more):
                    if more:
                        lows(U0 + d + 1)
                    for m in range(2):
                        dve.wait_ge(evac, 2 * (U0 + d) + m + 1)
                        if half_ == 0:
                            dve.wait_ge(acc_in, 16)
                        dst = acc[:, ds(2 * d + m, 1), :].squeeze(1)
                        dve.tensor_tensor(dst, dst, tmp[:, m, :], ALU.add).then_inc(tmp_used, 1)
                with dve.Fori(0, 8 if not half_ else 7) as d:
                    out_unit(d, True)
                dve.drain()
                if half_:
                    out_unit(7, False)
            dve.drain()
            dve.sem_inc(acc_done, 2 * KT)
            dve.wait_ge(rb_rt, 1)
            dve.reciprocal(rb1[:], rb1[:])
            dve.drain()
            for d in range(KT):
                dve.scalar_tensor_tensor(res[:, d, NM:L], acc[:, d, :], par[:, 0, PR_FINAL + d:PR_FINAL + d + 1], rb1[:],
                                         ALU.mult, ALU.mult)
                dve.drain()
            dve.sem_inc(res_done, 1)

            def norm(n, g, b):
                dve.wait_ge(ln_mean, n + 1)
                for d in range(KT):
                    dve.scalar_tensor_tensor(two(res[:, d, :]), halves(4), -1.0 / D, two(res[:, d, :]), ALU.mult, ALU.add)\
                       .then_inc(ln_c, 1)
                dve.wait_ge(ln_rt, n + 1)
                dve.reciprocal(lrb[:], lrb[:])
                dve.drain()
                for d in range(KT + 1):
                    if d < KT:
                        dve.scalar_tensor_tensor(lt[:, d % 2, :], res[:, d, :], g(d), lrb[:], ALU.mult, ALU.mult).then_inc(ln_t, 1)
                    if d > 0:
                        e = d - 1
                        dve.wait_ge(xh_done, norm_fill(n) + e + 1)
                        dve.scalar_tensor_tensor(xl[:, e, :], lt[:, e % 2, :], b(e), f(xh[:, e, :]), ALU.add, ALU.subtract)\
                           .then_inc(x_ready, 1)
                        dve.drain()

            norm_fill = lambda n: (3 + 2 * n) * KT

            dve.wait_ge(meta_ok, 1)
            norm(0, lambda d: par[:, 1, PR_LNG - P + d:PR_LNG - P + d + 1], lambda d: par[:, 1, PR_LNB - P + d:PR_LNB - P + d + 1])
            dve.drain()
            dve.memset(cra[:, 0:TAPS - 1], 0.0)
            dve.memset(rx[:, 0:RTAPS - 1], 0.0)
            dve.memset(wa[:], 0.0)
            dve.memset(wx[:], 0.0)
            dve.memset(small[:, 16:41], 1.0)
            dve.drain()
            dve.sem_inc(pads_ok, 1)
            dve.sem_inc(s_taken, 2)

            with dve.Fori(0, LAYERS) as l:
                U = U_LAYER + N_LAYER * l
                lows(U)
                lows(U + O_V)
                dve.wait_ge(lam_exp, l + 1)
                z, w, q, p = small[:, 41:45], small[:, 45:49], small[:, 49:53], small[:, 53:57]
                log1p(w, q, p, z)
                dve.tensor_scalar(z, plr(PL_LAM, CT), -1.0, 0.0, ALU.mult, ALU.max)
                dve.drain()
                dve.scalar_tensor_tensor(z, p, 2.0, z, ALU.mult, ALU.add)
                dve.drain()
                dve.tensor_scalar(w, z, -8.0, None, ALU.mult)
                dve.tensor_scalar(q, z, 8.0, None, ALU.mult).then_inc(sp_ok, 1)
                dve.wait_ge(shape_in, 16 * (l + 1))
                dve.wait_ge(sink_in, 16 * (l + 1))
                lows(U + O_V + 1)

                with dve.Fori(0, NKV) as g:
                    V = U + O_GRP + 4 * g
                    G = NKV * l + g
                    A = NH * l + GROUP * g
                    W3 = NM + 2 * BLK

                    def scored(i, n):
                        dve.wait_ge(s_done, 4 * A + 4 * i + n + 1)
                        w = W3 if n else NM + BLK
                        ins = dve.scalar_tensor_tensor(pb[:, i % 2, n * W3:n * W3 + w], ps[:, 4 + n % 2, 0:w],
                                                       float(HD) ** -0.5, mas if n else ma0, ALU.mult, ALU.add)
                        if n == 0:
                            ins = dve.scalar_tensor_tensor(pb[0:NM, i % 2, 4 * W3:4 * W3 + NM], ps[0:NM, 4, 160:160 + NM],
                                                           float(HD) ** -0.5, mca[0:NM, :], ALU.mult, ALU.add)
                        ins.then_inc(s_taken, 1)
                        if n == 3:
                            dve.drain()
                            dve.tensor_reduce(small[:, 16:17], pb[:, i % 2, 0:NM + BLK], AX.X, ALU.max)
                            dve.tensor_reduce(small[:, 17:20], pb[:, i % 2, W3:4 * W3].rearrange("p (n w) -> p n w", w=W3), AX.X, ALU.max)
                            dve.tensor_reduce(small[0:NM, 20:21], pb[0:NM, i % 2, 4 * W3:4 * W3 + NM], AX.X, ALU.max)
                            dve.drain()
                            dve.tensor_scalar(small[:, 21:26], small[:, 16:21], small[:, ds(GROUP * g + i, 1)], -1.0,
                                              ALU.max, ALU.mult).then_inc(att_max, 1)

                    def summed(i):
                        dve.wait_ge(att_exp, A + i + 1)
                        dve.tensor_tensor(small[:, 36:41], small[:, 26:31], small[:, 31:36], ALU.add)
                        dve.drain()
                        dve.reciprocal(small[:, 36:41], small[:, 36:41]).then_inc(att_sum, 1)

                    def taps(a0, a1):
                        dve.drain()
                        if a0 == PTAPS:
                            dve.wait_ge(c_gated, G + 1)
                        for j in range(a0, a1):
                            wj = pl[:, 0, ds(CT * j + g, 1)]
                            if j == PTAPS:
                                dve.tensor_scalar(cacc[:], cra[:, j:j + L], wj, pl[:, 0, ds(PL_DWB + g, 1)], ALU.mult, ALU.add)
                            else:
                                dve.scalar_tensor_tensor(cacc[:], cra[:, j:j + L], wj, cacc[:], ALU.mult, ALU.add)
                            dve.drain()

                    def attended(c):
                        dve.wait_ge(pv_done, A + 2 * c + 2)
                        dve.wait_ge(evac, 2 * (V + 2) + c + 1)
                        y = y2[:, ds(CT + 2 * g + c, 1), :].squeeze(1)
                        dve.tensor_tensor(y[:, NM:L], ps[:, 7, :], agt[:, c, NM:L], ALU.mult)
                        dve.tensor_tensor(y[:, 0:NM], mo[:], agt[:, c, 0:NM], ALU.mult)\
                           .then_inc(o_taken, 1)

                    def rope(t):
                        src = qrw[:, t, :] if t < 2 else krd[:, ds(g, 1), :].squeeze(1)
                        dst = qg[:, t, :] if t < 2 else kg[:]
                        dve.drain()
                        dve.wait_ge(rot_mm, 3 * G + t + 1)
                        dve.tensor_tensor(two(t1[:]), halves(4 + 2 * (t % 2)), two(sin), ALU.mult)
                        dve.tensor_tensor(dst, src, cos, ALU.mult)
                        dve.drain()
                        dve.tensor_tensor(dst, dst, t1[:], ALU.add).then_inc(rope_done, 1)

                    lows(V + 1)
                    rope(0)
                    rope(1)
                    rope(2)
                    scored(0, 0)
                    scored(0, 1)
                    low(V + 2, 0)
                    scored(0, 2)
                    low(V + 2, 1)
                    scored(0, 3)
                    low(V + 2, 2)
                    scored(1, 0)
                    summed(0)
                    low(V + 2, 3)
                    scored(1, 1)
                    taps(PTAPS, 11)
                    scored(1, 2)
                    taps(11, 12)
                    scored(1, 3)
                    taps(12, 13)
                    scored(2, 0)
                    summed(1)
                    scored(2, 1)
                    low(V + 3, 0)
                    scored(2, 2)
                    low(V + 3, 1)
                    taps(13, 14)
                    scored(2, 3)
                    low(V + 3, 2)
                    scored(3, 0)
                    summed(2)
                    low(V + 3, 3)
                    scored(3, 1)
                    taps(14, 15)
                    scored(3, 2)
                    attended(0)
                    taps(15, 16)
                    scored(3, 3)
                    taps(16, 17)
                    summed(3)
                    dve.drain()
                    dve.wait_ge(pt_done, 4 * A + 12)
                    dve.wait_ge(evac, 2 * (V + 3) + 1)
                    rwc = lambda j: pl[:, 1, ds(PL_RW - P + CT * j + g, 1)]
                    dve.tensor_scalar(rcv[:], rx[:, 0:L], rwc(0), pl[:, 1, ds(PL_RB - P + g, 1)], ALU.mult, ALU.add)
                    for j in range(1, RTAPS):
                        dve.drain()
                        ins = dve.scalar_tensor_tensor(rcv[:], rx[:, j:j + L], rwc(j), rcv[:], ALU.mult, ALU.add)
                    ins.then_inc(r_conved, 1)
                    low(V + 4, 0)
                    taps(17, 18)
                    low(V + 4, 1)
                    taps(18, 19)
                    low(V + 4, 2)
                    taps(19, 20)
                    low(V + 4, 3)
                    attended(1)
                    taps(20, 22)
                    dve.drain()
                    dve.wait_ge(r_act2, G + 1)
                    dve.tensor_tensor(rcv[:], rcv[:], rgx[:], ALU.mult)
                    dve.drain()
                    dve.tensor_tensor(rgx[:], rga[:], rga[:], ALU.mult)
                    dve.drain()
                    dve.scalar_tensor_tensor(rth[:], rgx[:], 1.0, rth[:], ALU.add, ALU.mult).then_inc(r_w, 1)
                    taps(22, 24)
                    dve.wait_ge(r_sqrt, G + 1)
                    dve.tensor_tensor(rcv[:], rcv[:], rth[:], ALU.mult)
                    dve.drain()
                    dve.tensor_tensor_scan(rth[:], rga[:], rcv[:], 0.0, ALU.mult, ALU.add)
                    dve.drain()
                    dve.wait_ge(evac, 2 * (V + 3) + 2)
                    dve.tensor_tensor(y2[:, ds(CT + 8 + g, 1), :].squeeze(1), rth[:], rgs[:], ALU.mult).then_inc(lru_done, 1)
                    taps(24, TAPS)
                    dve.wait_ge(c_part, G + 1)
                    ct = y2[:, ds(g, 1), :].squeeze(1)
                    dve.tensor_tensor(ct, ct, cacc[:], ALU.add).then_inc(c_taken, 1)

                C = U + O_CG
                dve.drain()
                dve.wait_ge(cn_mean, l + 1)
                for d in range(CT):
                    dve.scalar_tensor_tensor(two(y2[:, d, :]), halves(4), -1.0 / CW, two(y2[:, d, :]), ALU.mult, ALU.add)\
                       .then_inc(cn_c, 1)
                lows(C + 1)
                dve.wait_ge(cn_rt, l + 1)
                dve.reciprocal(lrb[:], lrb[:])
                dve.drain()
                for d in range(CT):
                    dve.scalar_tensor_tensor(y2[:, d, :], y2[:, d, :], plc(PL_CLG + d), lrb[:], ALU.mult, ALU.mult).then_inc(cn_t, 1)
                for d in range(CT):
                    dve.wait_ge(cn_hi, CT * l + d + 1)
                    dve.tensor_tensor(clo[:, d, :], y2[:, d, :], f(chi[:, d, :]), ALU.subtract).then_inc(c_ready, 1)
                lows(C + 2)
                W = U + O_PW
                dve.wait_ge(evac, 2 * W + 2)
                dve.tensor_tensor(y2[:, 0:CT, :], y2[:, 0:CT, :], cgt[:], ALU.mult).then_inc(y_conv, 1)
                dve.drain()
                lows(W + 1)
                with dve.Fori(0, KT) as k:
                    dve.tensor_tensor(res[:, ds(k, 1), :], f(xh[:, ds(k, 1), :]), f(xl[:, ds(k, 1), :]), ALU.add).then_inc(res_saved, 1)
                    dve.drain()
                    dve.wait_ge(xh_done, norm_fill(l) + KT + k + 1)
                    dve.tensor_tensor(xl[:, ds(k, 1), :], y2[:, ds(k, 1), :], f(xh[:, ds(k, 1), :]), ALU.subtract).then_inc(x_ready, 1)

                def out_unit(d, more):
                    if more:
                        lows(U + O_OUT + d + 1)
                    for m in range(2):
                        dve.wait_ge(evac, 2 * (U + O_OUT + d) + m + 1)
                        dst = res[:, ds(2 * d + m, 1), :].squeeze(1)
                        dve.scalar_tensor_tensor(dst, dst, ALPHA, tmp2[:, m, :], ALU.mult, ALU.add).then_inc(tmp_used, 1)
                with dve.Fori(0, 7) as d:
                    out_unit(d, True)
                out_unit(7, False)
                dve.drain()
                dve.sem_inc(z_done, KT)
                norm(l + 1, lambda d: plc(PL_PG + d), lambda d: plc(PL_PB + d))


def shape_constants():
    c = np.zeros((P, K_ALL), np.float32)
    i = np.arange(P)
    c[:, K_IDENT:K_IDENT + P] = np.eye(P)
    c[:, K_ONES:K_ONES + P] = 1.0
    c[:, K_TRI:K_TRI + P] = i[:, None] <= i[None, :]
    half = HD // 4 // 2
    for o in (0, HD):
        for d in range(half):
            c[o + half + d, K_ROT + o + d] = -1.0
            c[o + d, K_ROT + o + half + d] = 1.0
    neg = np.float32(-1e30)
    own = np.where(i[None, :] <= i[:, None], np.float32(0), neg)
    prev = np.where(i[None, :] > i[:, None], np.float32(0), neg)
    c[:, K_MASK0 + NM:K_MASK] = own
    c[:, K_MASK + NM:K_MASK + NM + BLK] = prev
    c[:, K_MASK + NM + BLK:K_CAUS] = own
    c[:, K_CAUS:K_COS] = own[:, 0:NM]
    freq = np.float32(500000.0) ** (-np.arange(half, dtype=np.float32) / np.float32(half))
    ang = np.arange(L, dtype=np.float32)[:, None] * freq.astype(np.float32)[None, :]
    c[:, K_COS:K_SIN] = 1.0
    for o in (0, HD):
        for q in (0, half):
            c[o + q:o + q + half, K_COS:K_SIN] = np.cos(ang).T
            c[o + q:o + q + half, K_SIN:K_ALL] = np.sin(ang).T
    return c


NAMES = ["x", "norm_w", "w_in", "conv_w", "conv_b", "b_igate", "b_fgate", "mlstm_norm_w", "sgu_norm_w", "sgu_norm_b",
         "w_spatial", "b_spatial", "w_out", "final_norm_w", "meta_tokens_2", "ln_in_g_2", "ln_in_b_2", "w_in_2",
         "conv_dw_w_2", "conv_dw_b_2", "conv_ln_g_2", "conv_ln_b_2", "conv_pw_w_2", "conv_pw_b_2", "attn_sinks_2",
         "lru_conv_w_2", "lru_conv_b_2", "lru_wa_2", "lru_ba_2", "lru_wx_2", "lru_bx_2", "lru_lambda_2", "w_out_2",
         "ln_post_g_2", "ln_post_b_2"]


def kernel(**inputs):
    import concourse.bacc as bacc
    from concourse.bass_utils import run_bass_kernel_spmd

    nc = bacc.Bacc("TRN2", target_bir_lowering=False, num_devices=1)
    arrays, aps = {}, {}
    for name in NAMES + ["shape_constants"]:
        v = shape_constants() if name == "shape_constants" else np.ascontiguousarray(inputs[name])
        arrays[f"in_{name}"] = v
        aps[name] = nc.dram_tensor(f"in_{name}", v.shape, mybir.dt.from_np(v.dtype), kind="ExternalInput").ap()
    out = nc.dram_tensor("out", (1, S, D), F32, kind="ExternalOutput").ap()
    program(nc, aps, out)
    return run_bass_kernel_spmd(nc, [arrays], core_ids=[0]).results[0]["out"]
```

```python
from contextlib import ExitStack

import numpy as np

import concourse.bass as bass
from concourse import mybir

F32 = mybir.dt.float32
F32R = mybir.dt.float32r
ACT = mybir.ActivationFunctionType
ALU = mybir.AluOpType
AX = mybir.AxisListType
ds = bass.ds

P = 128
D = 2048
KT = D // P
S = 512
ST = S // P
H = 8
DV = D // H
QK = H * P
EPS = 1e-6
C_Q, C_K = 0, QK
C_V, C_O, C_Z = 2 * QK, 2 * QK + D, 2 * QK + 2 * D
C_I = 2 * QK + 3 * D
C_F = C_I + H
C_U = C_F + H
C_VG, C_ZG = C_U + D, C_U + 2 * D

NM = 16
L = NM + S
LH = L // 2
LAYERS = 2
CW = D // 4
CT = CW // P
TAPS = 31
HD = 64
NKV = 4
GROUP = 4
NH = NKV * GROUP
BLK = 128
LN_EPS = 1e-5
ALPHA = (2.0 * LAYERS) ** 0.25
RTAPS = 4
D_CV, D_CG, D_CGATE = 0, CW, 2 * CW
D_Q = 3 * CW
D_K = D_Q + NH * HD
D_V = D_K + NKV * HD
D_AG = D_V + NKV * HD
D_RX = D_AG + NH * HD
D_RG = D_RX + CW

U_GATE = 0
U_SGU = 1
U_MLSTM = U_SGU + 3 * H
U_OUT_M = U_MLSTM + 4 * H
U_OUT_G = U_OUT_M + 8
U_LAYER = U_OUT_G + 8
N_LAYER = 29
O_K, O_V, O_GRP, O_CG, O_PW, O_OUT = 0, 1, 2, 18, 20, 21

Y_ATT, Y_LRU, Y_CONV = 0, 8, 12

K_IDENT, K_ONES, K_TRI, K_ROT = 0, P, 2 * P, 3 * P
K_MASK0 = 4 * P
K_MASK = K_MASK0 + NM + BLK
K_CAUS = K_MASK + NM + 2 * BLK
K_COS = K_CAUS + NM
K_SIN = K_COS + L
K_ALL = K_SIN + L

PR_NORM, PR_CONVW, PR_CONVB, PR_MNORM, PR_FINAL = 0, 16, 80, 96, 112
PR_SGUW, PR_SGUB, PR_LNG, PR_LNB = 128, 144, 160, 176
PL_DW, PL_DWB = 0, TAPS * CT
PL_CLG, PL_CLB, PL_PWB = 128, 132, 136
PL_RW, PL_RB = 140, 156
PL_PG, PL_PB = PR_LNG, PR_LNB
PL_BA, PL_BX, PL_LAM = 192, 196, 200
PL_END = 204
ROWS1, ROWS_L2 = 64, PL_END - P

LOG1P = [1.0 / (2 * n + 1) for n in range(9)]


def program(nc, a, out):
    consts = a["shape_constants"]
    x_t = nc.dram_tensor("x_feature_major", (P, KT, S), F32, kind="Internal").ap()
    x_res = nc.dram_tensor("residual_stream", (P, KT, L), F32, kind="Internal").ap()
    gate_rows = nc.dram_tensor("gate_rows", (H, 2, S), F32, kind="Internal").ap()

    w_in = a["w_in"].rearrange("(k p) n -> p k n", p=P)
    w_out = a["w_out"].rearrange("(k p) n -> p k n", p=P)
    w_in2 = a["w_in_2"].rearrange("l (k p) n -> p (l k) n", p=P)
    w_out2 = a["w_out_2"].rearrange("l (k p) n -> p (l k) n", p=P)
    w_pw = a["conv_pw_w_2"].rearrange("l (k p) n -> p (l k) n", p=P)
    x_nat = a["x"].rearrange("o (i p) d -> p (o i) d", p=P)
    out_nat = out.rearrange("o (i p) d -> p (o i) d", p=P)

    with ExitStack() as ctx:
        base = (nc.sbuf_base + 31) // 32 * 32
        limit = nc.sbuf_top

        class Region:
            def __init__(self, at):
                self.at = at

            def take(self, name, shape, dt=F32):
                size = 4
                for n in shape[1:]:
                    size *= n
                t = nc.alloc_sbuf_tensor_at(name, shape, dt, offset=self.at)
                self.at += (size + 31) // 32 * 32
                assert self.at <= limit, (name, self.at - limit)
                return t

        r0 = Region(base)
        ps = ctx.enter_context(nc.psum_tensor("ps", [P, 8, 512], F32))
        xh = r0.take("x_high", [P, KT, L], F32R)
        xl = r0.take("x_low", [P, KT, L], F32R)
        wh = r0.take("w_high", [P, 4, 4, 256], F32R)
        wl = r0.take("w_low", [P, 4, 4, 256], F32R)
        raw = r0.take("w_raw", [P, 4, 4, 256])
        ident = r0.take("ident", [P, P])
        ones = r0.take("ones", [P, P])
        tri_at = r0.at
        tri = r0.take("tri", [P, P])
        par = r0.take("par", [P, 2, P])
        pl = par
        small = r0.take("small", [P, 64])
        at = r0.take("a_t", [P, ST, H])
        big = r0.at

        r1 = Region(big)
        yg = r1.take("y_g", [P, KT, S])
        ym_at = r1.at
        ym = r1.take("y_m", [P, KT, S])
        acc = nc.alloc_sbuf_tensor_at("acc", [P, KT, S], F32, offset=ym_at)
        work = r1.at
        xs = nc.alloc_sbuf_tensor_at("x_scaled", [P, ST, D], F32, offset=big)
        xn = nc.alloc_sbuf_tensor_at("x_natural", [P, ST, D], F32, offset=ym_at)
        rp = Region(work)
        stage = rp.take("x_stage", [P, KT // 2, S])
        prow = rp.take("par_rows", [P, 2, P])
        ra = Region(ym_at)
        ws = ra.take("w_spatial_natural", [P, H, P])
        wst = ra.take("w_spatial_t", [P, H, P])
        rsb = ra.take("w_spatial_rowsum", [P, H, P])
        bsp = ra.take("b_spatial_bc", [P, H, P])
        svr = ra.take("sgu_bias", [P, 2, P])
        sv = ra.take("sgu_v", [P, 2, S])
        li = ra.take("log_i", [8, S])
        xf = ra.take("f_pre", [8, S])
        gz = ra.take("gate_z", [8, S])
        gw = ra.take("gate_w", [8, S])
        gq = ra.take("gate_q", [8, S])
        assert ra.at <= work
        rb = Region(work)
        vg = rb.take("v_gelu", [P, ST, DV])
        vn = rb.take("v_normed", [P, ST, DV])
        ug = rb.take("u_gelu", [P, 2, S])
        zg = rb.take("z_silu_g", [P, 2, S])
        gp = rb.take("gate_p", [8, S])
        gout = rb.take("gate_out", [8, 2, S])
        rc = Region(work)
        qc = rc.take("q_head", [P, S])
        kc = rc.take("k_head", [P, S])
        vv = rc.take("v_head", [P, ST, DV])
        og = rc.take("o_gate", [P, 2, S])
        zz = rc.take("z_silu_m", [P, S])
        bc = rc.take("gate_bc", [P, 2, S])
        pj_at = rc.at
        pj = rc.take("p_tiles", [P, 5 * 256])
        sq = nc.alloc_sbuf_tensor_at("square", [P, 2, S], F32, offset=pj_at)
        rd = nc.alloc_sbuf_tensor_at("recip_bc", [P, S], F32, offset=rc.at)
        cr = rc.take("conv_raw", [P, 4 + S])
        PTAPS = 9
        POFF = [0, 512, 896, 1152]
        ro = Region(work)
        tmp = ro.take("out_tmp", [P, 2, S])

        r2 = Region(big)
        res = r2.take("residual", [P, KT, L])
        y2_at = r2.at
        y2 = r2.take("y_layer", [P, KT, L])
        work2 = r2.at
        rr = Region(big)
        krw = nc.alloc_sbuf_tensor_at("k_raw", [P, 2, L], F32, offset=big)
        qrw = rr.take("q_raw", [P, 2, L])
        krd = rr.take("k_raw_twice", [P, NKV, L])
        v2 = rr.take("v_tokens", [P, ST + 1, NKV * HD])
        qg = rr.take("q_group", [P, 2, L])
        kg = rr.take("k_group", [P, L])
        vgr = rr.take("v_group", [P, ST + 1, HD])
        shape_at = rr.at
        kshape = rr.take("shape_constants", [P, K_ALL - K_ROT])
        rot = kshape[:, 0:P]
        ma0 = kshape[:, K_MASK0 - K_ROT:K_MASK - K_ROT]
        mas = kshape[:, K_MASK - K_ROT:K_CAUS - K_ROT]
        mca = kshape[:, K_CAUS - K_ROT:K_COS - K_ROT]
        cos = kshape[:, K_COS - K_ROT:K_SIN - K_ROT]
        sin = kshape[:, K_SIN - K_ROT:K_ALL - K_ROT]
        mo = rr.take("meta_out", [P, NM])
        assert rr.at <= y2_at, rr.at - y2_at
        chi = nc.alloc_sbuf_tensor_at("c_high", [P, CT, L], F32R, offset=big)
        clo = nc.alloc_sbuf_tensor_at("c_low", [P, CT, L], F32R, offset=big + CT * L * 4)
        cgt = nc.alloc_sbuf_tensor_at("c_gate_silu", [P, CT, L], F32, offset=big + 2 * CT * L * 4)
        prow2 = nc.alloc_sbuf_tensor_at("par_rows_layer", [P, 2, P], F32, offset=work2)
        rw = Region(work2)
        pb = rw.take("p_block", [P, 2, 4 * (NM + 2 * BLK) + NM])
        pts = rw.take("p_transposed", [P, 2, 3 * BLK])
        agt = rw.take("a_gate_silu", [P, 2, L])
        ptm = rw.take("p_meta_transposed", [NM, NM])
        cra = rw.take("c_raw", [P, TAPS - 1 + L])
        t1 = rw.take("tmp1", [P, L])
        rx = rw.take("rx_raw", [P, RTAPS + L])
        cacc = rw.take("c_partial", [P, L])
        wa = nc.alloc_sbuf_tensor_at("w_a_diag", [P, P], F32, offset=tri_at)
        wx = rw.take("w_x_diag", [P, P])
        half = (4 * (NM + 2 * BLK) + NM) * 4
        assert 2 * L * 4 <= half
        rcv = nc.alloc_sbuf_tensor_at("r_conv", [P, L], F32, offset=work2)
        rga = nc.alloc_sbuf_tensor_at("r_gate_a", [P, L], F32, offset=work2 + L * 4)
        rgx = nc.alloc_sbuf_tensor_at("r_gate_x", [P, L], F32, offset=work2 + half)
        rth = nc.alloc_sbuf_tensor_at("r_tanh", [P, L], F32, offset=work2 + half + L * 4)
        rgs = t1
        rn = Region(ro.at)
        mnat = nc.alloc_sbuf_tensor_at("meta_natural", [NM, D], F32, offset=rn.at)
        lrb = rn.take("norm_scale_bc", [P, L])
        tmp2 = rn.take("out_tmp_layer", [P, 2, L])
        mub = rn.take("norm_mean_bc", [P, L])
        dif = rn.take("norm_difference", [P, L])
        dsq = rn.take("norm_square", [P, L])
        dsum = rn.take("norm_sum", [P, L])
        dsqs = rn.take("norm_square_sum", [P, L])
        ssum = rn.take("rms_square_sum", [P, L])
        csq = nc.alloc_sbuf_tensor_at("c_square", [P, CT, L], F32, offset=big + 3 * CT * L * 4)
        outn = nc.alloc_sbuf_tensor_at("out_natural", [P, 4, ST, D // 4], F32, offset=big)

        def sem(name):
            return ctx.enter_context(nc.semaphore(name))

        raw_full = [sem(f"raw_full{j}") for j in range(4)]
        hi_ready = sem("hi_ready")
        lo_ready = sem("lo_ready")
        piece_used = sem("piece_used")
        pass0_done = sem("pass0_done")
        evac = sem("evac")
        xh_done = sem("xh_done")
        x_ready = sem("x_ready")
        const_in, par_in, xn_in = sem("const_in"), sem("par_in"), sem("xn_in")
        par_tr, par_ok = sem("par_tr"), sem("par_ok")
        x_ss, x_var, x_sd, xs_ready = sem("x_ss"), sem("x_var"), sem("x_sd"), sem("xs_ready")
        tr_raw, tr_raw_free, tr_sc = sem("tr_raw"), sem("tr_raw_free"), sem("tr_sc")
        x_stored = [sem(f"x_stored{i}") for i in range(KT // 2)]
        ws_in, ws_masked, wst_tr, wst_ok, rs_mm, rs_ok = (
            sem("ws_in"), sem("ws_masked"), sem("wst_tr"), sem("wst_ok"), sem("rs_mm"), sem("rs_ok"))
        g_z, g_m, g_em, at_tr, at_ok, gr_stored = (
            sem("g_z"), sem("g_m"), sem("g_em"), sem("at_tr"), sem("at_ok"), sem("gr_stored"))
        a_var, a_sd, vn_ready, sgu_done, sv_done, ug_used, yg_done = (
            sem("a_var"), sem("a_sd"), sem("vn_ready"), sem("sgu_done"), sem("sv_done"), sem("ug_used"), sem("yg_done"))
        bc_in, cq_done, qk_ready, s_mm, p_arg, p_exp, p_done = (
            sem("bc_in"), sem("cq_done"), sem("qk_ready"), sem("s_mm"), sem("p_arg"), sem("p_exp"), sem("p_done"))
        pv_m, den_abs, h_ready, sq_ready, ms_mm, rms_rt, zz_used, ym_done = (
            sem("pv_m"), sem("den_abs"), sem("h_ready"), sem("sq_ready"), sem("ms_mm"), sem("rms_rt"),
            sem("zz_used"), sem("ym_done"))
        acc_in, tmp_used, meta_in, meta_tr, meta_ok = (
            sem("acc_in"), sem("tmp_used"), sem("meta_in"), sem("meta_tr"), sem("meta_ok"))
        ln_local, ln_mean, mu_ok, ln_m2, ln_mm, ln_rt, ln_sub, ln_t, y_full = (
            sem("ln_local"), sem("ln_mean"), sem("mu_ok"), sem("ln_m2"), sem("ln_mm"), sem("ln_rt"), sem("ln_sub"),
            sem("ln_t"), sem("y_full"))
        res_out = sem("res_out")
        res_in = [sem(f"res_in{c}") for c in range(4)]
        shape_in, pl_in, pl_tr, pl_ok, sink_in, krd_in = (
            sem("shape_in"), sem("pl_in"), sem("pl_tr"), sem("pl_ok"), sem("sink_in"), sem("krd_in"))
        rot_mm, rope_done, vgr_ready = sem("rot_mm"), sem("rope_done"), sem("vgr_ready")
        s_done, s_taken, att_max, att_exp, p_ready = (
            sem("s_done"), sem("s_taken"), sem("att_max"), sem("att_exp"), sem("p_ready"))
        pt_done, pt_evac, pv_done, o_taken = sem("pt_done"), sem("pt_evac"), sem("pv_done"), sem("o_taken")
        c_taken, rw_in, r_conved, r_mm, r_act, r_act2, r_w, r_sqrt, lru_done, pads_ok = (
            sem("c_taken"), sem("rw_in"), sem("r_conved"), sem("r_mm"), sem("r_act"), sem("r_act2"), sem("r_w"), sem("r_sqrt"),
            sem("lru_done"), sem("pads_ok"))
        zeros_ok = sem("zeros_ok")
        c_gated, c_part, att_sum = sem("c_gated"), sem("c_part"), sem("att_sum")
        lam_exp, sp_ok = sem("lam_exp"), sem("sp_ok")
        cn_mean, cn_c, cn_sq, cn_mm, cn_rt, cn_t, cn_hi, c_ready = (
            sem("cn_mean"), sem("cn_c"), sem("cn_sq"), sem("cn_mm"), sem("cn_rt"), sem("cn_t"),
            sem("cn_hi"), sem("c_ready"))
        pw_done, y_conv = sem("pw_done"), sem("y_conv")
        fin_tr, fin_act, fin_dve, out_st = sem("fin_tr"), sem("fin_act"), sem("fin_dve"), sem("out_st")

        halves = lambda b: ps[:, b:b + 2, 0:LH]
        two = lambda t: t.rearrange("p (a n) -> p a n", a=2)
        f = lambda t: t.bitcast(F32)
        plr = lambda c, n: pl[:, c // P, c % P:c % P + n]
        plc = lambda c: pl[:, c // P, c % P:c % P + 1]
        shift = POFF

        block = ctx.enter_context(nc.Block())

        @block.sync
        def _(sp):
            def load(U, src, pair=None, wide=256):
                for j in range(4):
                    if not (isinstance(U, int) and U == 0):
                        sp.wait_ge(lo_ready, 4 * U - 3 + j)
                    for i in range(2):
                        if pair:
                            sp.dma_start(raw[:, j, :, i * P:(i + 1) * P], pair[i](j, slice(0, 4))).then_inc(raw_full[j], 16)
                        else:
                            sp.dma_start(raw[:, j, 2 * i:2 * i + 2, 0:wide], src(j, slice(2 * i, 2 * i + 2))).then_inc(raw_full[j], 16)

            def cols(w, col, n=256, row=0):
                return lambda j, r: w[:, ds(row + 4 * j + r.start, r.stop - r.start), ds(col, n)]

            for i in range(ST):
                sp.dma_start(xn[:, i, :], x_nat[:, i, :]).then_inc(xn_in, 16)
            load(U_GATE, None, (cols(w_in, C_I, P), cols(w_in, C_F, P)))
            with sp.Fori(0, H) as h:
                for n, c in enumerate((C_VG, C_U, C_ZG)):
                    load(U_SGU + 3 * h + n, cols(w_in, c + DV * h))
            with sp.Fori(0, H) as h:
                U = U_MLSTM + 4 * h
                load(U, None, (cols(w_in, C_Q + P * h, P), cols(w_in, C_K + P * h, P)))
                for n, c in enumerate((C_V, C_O, C_Z)):
                    load(U + 1 + n, cols(w_in, c + DV * h))
            with sp.Fori(0, 8) as d:
                load(U_OUT_M + d, cols(w_out, 256 * d))
            with sp.Fori(0, 8) as d:
                load(U_OUT_G + d, cols(w_out, 256 * d, row=KT))
            with sp.Fori(0, LAYERS) as l:
                U = U_LAYER + N_LAYER * l
                load(U + O_K, cols(w_in2, D_K, row=KT * l))
                load(U + O_V, cols(w_in2, D_V, row=KT * l))
                sp.wait_ge(evac, 2 * (U + O_K) + 2)
                for g in range(NKV):
                    for o in (0, HD):
                        s0 = g % 2 * HD
                        sp.dma_start(krd[o:o + HD, g, :], krw[s0:s0 + HD, g // 2, :]).then_inc(krd_in, 16)
                with sp.Fori(0, NKV) as g:
                    V = U + O_GRP + 4 * g
                    load(V, cols(w_in2, D_Q + 256 * g, row=KT * l))
                    load(V + 1, None, (cols(w_in2, D_CV + P * g, P, KT * l), cols(w_in2, D_CG + P * g, P, KT * l)))
                    load(V + 2, cols(w_in2, D_AG + 256 * g, row=KT * l))
                    load(V + 3, None, (cols(w_in2, D_RX + P * g, P, KT * l), cols(w_in2, D_RG + P * g, P, KT * l)))
                with sp.Fori(0, 2) as n:
                    load(U + O_CG + n, cols(w_in2, D_CGATE + 256 * n, row=KT * l))
                load(U + O_PW, lambda j, r: w_pw[:, ds(CT * l + r.start, 2), j * P:(j + 1) * P], wide=P)
                with sp.Fori(0, 8) as d:
                    load(U + O_OUT + d, lambda j, r: w_out2[:, ds(KT * l + (4 * j + CT) % KT + r.start, r.stop - r.start),
                                                            ds(256 * d, 256)])
            for q in range(4):
                sp.wait_ge(fin_act, 2 * q + 2)
                sp.wait_ge(fin_dve, 2 * q + 2)
                sp.dma_start(out_nat[:, :, q * 512:(q + 1) * 512], outn[:, q, :, :]).then_inc(out_st, 16)
            sp.wait_ge(out_st, 16 * 4)

        @block.gpsimd
        def _(pool):
            for n, c in ((ident, K_IDENT), (ones, K_ONES), (tri, K_TRI)):
                pool.dma_start(n[:], consts[:, c:c + P]).then_inc(const_in, 16)
            row = 0
            for name, n in (("norm_w", 16), ("conv_w", 64), ("conv_b", 16), ("mlstm_norm_w", 16), ("final_norm_w", 16),
                            ("sgu_norm_w", 16), ("sgu_norm_b", 16), ("ln_in_g_2", 16), ("ln_in_b_2", 16)):
                v = a[name]
                v = v.rearrange("j (t p) -> (j t) p", p=P) if len(v.shape) == 2 else v.rearrange("(t p) -> t p", p=P)
                pool.dma_start(prow[row % P:row % P + n, row // P, :], v).then_inc(par_in, 16)
                row += n
            pool.dma_start(small[0:8, 60:61], a["b_igate"].unsqueeze(1)).then_inc(par_in, 16)
            pool.dma_start(small[0:8, 61:62], a["b_fgate"].unsqueeze(1)).then_inc(par_in, 16)
            for d in range(KT):
                pool.wait_ge(tr_raw_free, d + 1)
                pool.dma_start(x_t[:, d, :], stage[:, d % 8, :]).then_inc(x_stored[d % 8], 16)
            pool.wait_ge(x_ready, KT)
            pool.dma_start(ws[:], a["w_spatial"].rearrange("h t s -> t h s")).then_inc(ws_in, 16)
            pool.dma_start(bsp[:], a["b_spatial"].partition_broadcast(P)).then_inc(ws_in, 16)
            pool.wait_ge(ws_in, 32)
            pool.affine_select(out=ws[:], in_=ws[:], compare_op=ALU.is_ge, fill=0.0, base=0,
                               pattern=[[0, H], [-1, P]], channel_multiplier=1).then_inc(ws_masked, 1)
            pool.wait_ge(g_em, 1)
            pool.dma_start(gate_rows, gout[:]).then_inc(gr_stored, 16)
            pool.wait_ge(gr_stored, 16)
            pool.wait_ge(yg_done, H)
            with pool.Fori(0, H) as h:
                pool.wait_ge(h_ready, h)
                pool.dma_start(bc[:], gate_rows[ds(h, 1)].squeeze(0).partition_broadcast(P)).then_inc(bc_in, 16)
            pool.wait_ge(x_ready, 2 * KT)
            for i in range(KT // 2):
                pool.wait_ge(x_stored[i], 16 * 2)
            pool.dma_start(acc[:], x_t).then_inc(acc_in, 16)
            pool.dma_start(mnat[:], a["meta_tokens_2"]).then_inc(meta_in, 16)

            def norm(n):
                pool.wait_ge(mu_ok, n + 1)
                for d in range(KT):
                    pool.tensor_tensor(res[:, d, :], res[:, d, :], mub[:], ALU.subtract).then_inc(ln_sub, 1)

            with pool.Fori(0, LAYERS) as l:
                norm(l)
                pool.wait_ge(pads_ok, 1)
                with pool.Fori(0, NKV) as g:
                    pool.wait_ge(r_mm, 2 * NKV * l + 2 * g)
                    for m, name in ((wa, "lru_wa_2"), (wx, "lru_wx_2")):
                        w = a[name].rearrange("l h i j -> i (l h) j")
                        for o in range(2):
                            pool.dma_start(m[o * HD:(o + 1) * HD, o * HD:(o + 1) * HD].unsqueeze(1),
                                           w[:, ds(8 * l + 2 * g + o, 1), :]).then_inc(rw_in, 16)
                    G = NKV * l + g
                    A = NH * l + GROUP * g
                    W3 = NM + 2 * BLK
                    ct = y2[:, ds(Y_CONV + g, 1), :].squeeze(1)

                    def normed(i):
                        pool.drain()
                        pool.wait_ge(att_sum, A + i + 1)
                        pool.tensor_tensor(pb[0:NM, i % 2, 4 * W3:4 * W3 + NM], pb[0:NM, i % 2, 4 * W3:4 * W3 + NM],
                                           small[0:NM, 40:41].broadcast_to([NM, NM]), ALU.mult)
                        p = pb[:, i % 2, 0:NM + BLK]
                        pool.tensor_tensor(p, p, small[:, 36:37].broadcast_to([P, NM + BLK]), ALU.mult)
                        p = pb[:, i % 2, W3:4 * W3].rearrange("p (n w) -> p n w", w=W3)
                        pool.tensor_tensor(p, p, small[:, 37:40].unsqueeze(2).broadcast_to([P, 3, W3]), ALU.mult)\
                            .then_inc(p_ready, 1)

                    def taps(a0, a1):
                        for j in range(a0, a1):
                            wj = pl[:, 0, ds(CT * j + g, 1)].broadcast_to([P, L])
                            if j == 0:
                                ins = pool.tensor_tensor(ct, cra[:, 0:L], wj, ALU.mult)
                            else:
                                pool.drain()
                                pool.tensor_tensor(t1[:], cra[:, j:j + L], wj, ALU.mult)
                                pool.drain()
                                ins = pool.tensor_tensor(ct, ct, t1[:], ALU.add)
                        return ins

                    pool.drain()
                    pool.wait_ge(res_out, 16 * l + 16)
                    pool.wait_ge(evac, 2 * (U_LAYER + N_LAYER * l + O_GRP + 4 * g + 1) + 2)
                    pool.tensor_tensor(cra[:, TAPS - 1:], cra[:, TAPS - 1:], agt[:, 0, :], ALU.mult).then_inc(c_gated, 1)
                    normed(0)
                    taps(0, 3)
                    normed(1)
                    taps(3, 6)
                    normed(2)
                    taps(6, PTAPS).then_inc(c_part, 1)
                    normed(3)
                pool.drain()
            norm(LAYERS)

        @block.tensor
        def _(pe):
            def three(dst, k, w, tok, m, j, kt, first, last):
                wc = slice(m * P, (m + 1) * P)
                pe.matmul(dst, wh[:, j, kt, wc], xh[:, k, tok], start=first, stop=False)
                pe.matmul(dst, wh[:, j, kt, wc], xl[:, k, tok], start=False, stop=False)
                return pe.matmul(dst, wl[:, j, kt, wc], xh[:, k, tok], start=False, stop=last)

            def three_t(dst, k, tok, j, kt, first, last):
                pe.matmul(dst, xh[:, k, tok], wh[:, j, kt, :], start=first, stop=False)
                pe.matmul(dst, xl[:, k, tok], wh[:, j, kt, :], start=False, stop=False)
                return pe.matmul(dst, xh[:, k, tok], wl[:, j, kt, :], start=False, stop=last)

            def begin(U, m):
                if not (isinstance(U, int) and U == 0):
                    pe.wait_ge(evac, 2 * U + m - 1)

            def end_piece(U, m, j, last):
                if m == 1:
                    last.then_inc(piece_used, 1)
                elif j == 3:
                    last.then_inc(pass0_done, 1)

            def arrive(U, m, j, fill, k=None):
                if m == 0:
                    pe.wait_ge(lo_ready, 4 * U + j + 1)
                    pe.wait_ge(x_ready, fill + 4 * (j + 1))

            def unit(U, fill, wide=False, after=(None, None), mid=(None, None), hook=None):
                for m in range(2):
                    begin(U, m)
                    for j in range(4):
                        arrive(U, m, j, fill)
                        for kt in range(4):
                            k = 4 * j + kt
                            if wide:
                                for q in range(2):
                                    last = three(ps[:, 2 * m + q, 0:LH], k, None, slice(q * LH, (q + 1) * LH), m, j, kt, k == 0, k == KT - 1)
                            else:
                                last = three(ps[:, m, :], k, None, slice(0, S), m, j, kt, k == 0, k == KT - 1)
                        end_piece(U, m, j, last)
                        if j == 1 and mid[m]:
                            mid[m]()
                        if hook:
                            hook(4 * m + j)
                    if after[m]:
                        after[m]()

            def unit_tokens(U, fill, first_token, groups, after=(None, None)):
                for m in range(2):
                    begin(U, m)
                    for i, (dst, tok) in enumerate(groups[m]):
                        for j in range(4):
                            if i == 0:
                                arrive(U, m, j, fill)
                            for kt in range(4):
                                k = 4 * j + kt
                                last = three_t(dst, k, slice(tok, tok + P), j, kt, k == 0, k == KT - 1)
                            if i == len(groups[m]) - 1:
                                end_piece(U, m, j, last)
                    if after[m]:
                        after[m]()

            tok1 = [[(ps[:, m, i * 256:(i + 1) * 256], (2 * m + i) * P) for i in range(2)] for m in range(2)]

            pe.wait_ge(const_in, 48)
            pe.wait_ge(xn_in, 16 * ST)
            for d in range(KT):
                if d >= 4:
                    pe.wait_ge(tr_raw_free, d - 3)
                for i in range(ST):
                    last = pe.transpose(ps[:, 4 + d % 4, i * P:(i + 1) * P], xn[:, i, d * P:(d + 1) * P], ident[:])
                last.then_inc(tr_raw, 1)
            pe.wait_ge(par_in, 16 * 11)
            pe.transpose(ps[:, 0, 0:P], prow[:, 0, :], ident[:])
            pe.transpose(ps[:, 1, 0:ROWS1], prow[0:ROWS1, 1, :], ident[0:ROWS1, 0:ROWS1]).then_inc(par_tr, 1)
            pe.wait_ge(xs_ready, 1)
            for d in range(KT):
                if d < 4:
                    pe.wait_ge(tr_raw_free, KT - 3 + d)
                else:
                    pe.wait_ge(x_ready, d - 3)
                for i in range(ST):
                    last = pe.transpose(ps[:, 4 + d % 4, i * P:(i + 1) * P], xs[:, i, d * P:(d + 1) * P], ident[:])
                last.then_inc(tr_sc, 1)

            unit(U_GATE, 0)
            pe.wait_ge(ws_masked, 1)
            for h in range(H):
                last = pe.transpose(ps[:, 4 + h // 4, h % 4 * P:(h % 4 + 1) * P], ws[:, h, :], ident[:])
            last.then_inc(wst_tr, 1)
            pe.wait_ge(wst_ok, 1)
            for q in range(2):
                last = pe.matmul(ps[:, 6 + q, :], ones[:], wst[:, 4 * q:4 * q + 4, :], start=True, stop=True)
            last.then_inc(rs_mm, 1)
            pe.wait_ge(rs_ok, 1)

            with pe.Fori(0, H) as h:
                U = U_SGU + 3 * h

                def mix():
                    pe.wait_ge(vn_ready, h + 1)
                    pe.wait_ge(sv_done, h)
                    for c in range(2):
                        for n in range(ST):
                            last = pe.matmul(ps[:, 4 + c, n * P:(n + 1) * P], vn[:, n, c * P:(c + 1) * P],
                                             wst[:, ds(h, 1), :], start=True, stop=True)
                    last.then_inc(sgu_done, 1)

                unit_tokens(U, 0, 0, tok1)
                unit(U + 1, 0, after=(mix, None))
                unit(U + 2, 0)

            pe.wait_ge(g_m, 1)
            for i in range(ST):
                last = pe.transpose(ps[:, 6, i * H:(i + 1) * H], gz[0:H, i * P:(i + 1) * P], ident[0:H, 0:H])
            last.then_inc(at_tr, 1)

            with pe.Fori(0, H) as h:
                U = U_MLSTM + 4 * h

                def scores():
                    pe.wait_ge(qk_ready, 2 * h + 2)
                    pe.wait_ge(ym_done, h + 1)
                    pe.wait_ge(at_ok, 1)
                    for j in range(ST):
                        pe.matmul(ps[:, 4 + j, 0:S - j * P], kc[:, j * P:(j + 1) * P], qc[:, j * P:S],
                                  start=True, stop=True).then_inc(s_mm, 1)

                def values():
                    pe.wait_ge(p_done, ST * h + ST)
                    pe.wait_ge(evac, 2 * U + 4)
                    for c in range(3):
                        for j in range(ST):
                            w = vv[:, j, c * P:(c + 1) * P] if c < 2 else ones[:]
                            last = pe.matmul(ps[:, 4 + c, j * P:S], w, pj[:, shift[j]:shift[j] + S - j * P],
                                             start=(j == 0), stop=(j == ST - 1))
                    last.then_inc(pv_m, 1)

                def squares():
                    pe.wait_ge(sq_ready, h + 1)
                    for c in range(2):
                        last = pe.matmul(ps[:, 7, :], ones[:], sq[:, c, :], start=(c == 0), stop=(c == 1))
                    last.then_inc(ms_mm, 1)

                unit(U, 0)
                unit_tokens(U + 1, 0, 0, tok1, after=(scores, None))
                unit(U + 2, 0, after=(values, None))
                unit(U + 3, 0, after=(squares, None))

            with pe.Fori(0, 8) as d:
                unit(U_OUT_M + d, KT)
            pe.wait_ge(meta_in, 16)
            for d in range(KT):
                last = pe.transpose(ps[:, 5, d * NM:(d + 1) * NM], mnat[:, d * P:(d + 1) * P], ident[0:NM, 0:NM])
            last.then_inc(meta_tr, 1)
            with pe.Fori(0, 8) as d:
                unit(U_OUT_G + d, 2 * KT)

            def sum_features(src, n, bank):
                for d in range(n):
                    for q in range(2):
                        last = pe.matmul(ps[:, bank + q, 0:LH], ones[:], src(d)[:, q * LH:(q + 1) * LH],
                                         start=(d == 0), stop=(d == n - 1))
                return last

            def norm(n):
                pe.wait_ge(ln_local, n + 1)
                sum_features(lambda d: dif[:], 1, 4).then_inc(ln_mean, 1)
                pe.wait_ge(ln_m2, n + 1)
                sum_features(lambda d: dsqs[:], 1, 6).then_inc(ln_mm, 1)

            with pe.Fori(0, LAYERS) as l:
                norm(l)
                U = U_LAYER + N_LAYER * l
                fill = (4 + 2 * l) * KT - KT
                unit(U + O_K, fill, wide=True)
                pe.wait_ge(pl_in, 16 * 12 * (l + 1))
                pe.transpose(ps[:, 4, 0:P], prow2[:, 0, :], ident[:])
                pe.transpose(ps[:, 5, 0:ROWS_L2], prow2[0:ROWS_L2, 1, :], ident[0:ROWS_L2, 0:ROWS_L2]).then_inc(pl_tr, 1)
                unit_tokens(U + O_V, fill, 0, [
                    [(ps[:, i // 2, i % 2 * 256:(i % 2 + 1) * 256], NM + i * P) for i in range(ST)],
                    [(ps[:, 2, 0:256], 0)]])
                with pe.Fori(0, NKV) as g:
                    V = U + O_GRP + 4 * g
                    G = NKV * l + g
                    A = NH * l + GROUP * g

                    def rotate(t):
                        if t == 0:
                            pe.wait_ge(evac, 2 * V + 2)
                            pe.wait_ge(shape_in, 16 * (l + 1))
                            pe.wait_ge(pl_ok, l + 1)
                            pe.wait_ge(krd_in, 128 * (l + 1))
                            pe.wait_ge(r_act, 2 * G)
                            pe.wait_ge(o_taken, 2 * G)
                        if t == 2:
                            pe.wait_ge(rope_done, 3 * G + 1)
                        for q in range(2):
                            rhs = (qrw[:, t, q * LH:(q + 1) * LH] if t < 2
                                   else krd[:, ds(g, 1), q * LH:(q + 1) * LH])
                            last = pe.matmul(ps[:, 4 + 2 * (t % 2) + q, 0:LH], rot, rhs, start=True, stop=True)
                        last.then_inc(rot_mm, 1)

                    def score(i, n):
                        o = i % 2 * HD
                        q = qg[o:o + HD, i // 2, :]
                        bank = 4 + n % 2
                        if n == 0 and i == 0:
                            pe.wait_ge(rope_done, 3 * G + 3)
                        pe.wait_ge(s_taken, 4 * A + 4 * i + n + 1)
                        tq = NM + n * BLK
                        if n < 2:
                            last = pe.matmul(ps[:, bank, 0:NM + (n + 1) * BLK], q[:, tq:tq + BLK],
                                             kg[o:o + HD, 0:NM + (n + 1) * BLK], start=True, stop=True)
                        else:
                            pe.matmul(ps[:, bank, 0:NM], q[:, tq:tq + BLK], kg[o:o + HD, 0:NM], start=True, stop=True)
                            last = pe.matmul(ps[:, bank, NM:NM + 2 * BLK], q[:, tq:tq + BLK],
                                             kg[o:o + HD, tq - BLK:tq + BLK], start=True, stop=True)
                        if n == 0:
                            last = pe.matmul(ps[0:NM, bank, 160:160 + NM], q[:, 0:NM], kg[o:o + HD, 0:NM],
                                             start=True, stop=True)
                        last.then_inc(s_done, 1)

                    def turn(i, n):
                        if n == 0:
                            pe.wait_ge(p_ready, A + i + 1)
                        pe.wait_ge(pt_evac, 4 * A + 4 * i + n)
                        if n == 1:
                            if i == 0:
                                pe.wait_ge(vgr_ready, G + 1)
                            o = i % 2 * HD
                            pe.matmul(ps[o:o + HD, 6, 3 * BLK + 2 * NM:3 * BLK + 3 * NM], vgr[0:NM, 0, :], ptm[:],
                                      start=True, stop=True)
                        c0 = n * (NM + 2 * BLK)
                        pe.transpose(ps[0:NM, 6, 0:BLK], pb[:, i % 2, c0:c0 + NM], ident[:])
                        if n > 0:
                            pe.transpose(ps[:, 6, BLK:2 * BLK], pb[:, i % 2, c0 + NM:c0 + NM + BLK], ident[:])
                            c0 += BLK
                        last = pe.transpose(ps[:, 6, 2 * BLK:3 * BLK], pb[:, i % 2, c0 + NM:c0 + NM + BLK], ident[:])
                        if n == 0:
                            cm = 4 * (NM + 2 * BLK)
                            last = pe.transpose(ps[0:NM, 6, 3 * BLK:3 * BLK + NM], pb[0:NM, i % 2, cm:cm + NM],
                                                ident[0:NM, 0:NM])
                        last.then_inc(pt_done, 1)

                    def value(i, n):
                        o = i % 2 * HD
                        if n == 0 and i % 2 == 0:
                            pe.wait_ge(o_taken, 2 * G + i // 2)
                        pe.wait_ge(pt_evac, 4 * A + 4 * i + n + 1)
                        dst = ps[o:o + HD, 7, n * BLK:(n + 1) * BLK]
                        pe.matmul(dst, vgr[0:NM, 0, :], pts[0:NM, n % 2, 0:BLK], start=True, stop=False)
                        if n > 0:
                            pe.matmul(dst, vgr[:, n, :], pts[:, n % 2, BLK:2 * BLK], start=False, stop=False)
                        last = pe.matmul(dst, vgr[:, n + 1, :], pts[:, n % 2, 2 * BLK:3 * BLK], start=False, stop=True)
                        if n == 3:
                            last.then_inc(pv_done, 1)

                    def step(k):
                        if k < 4 * GROUP:
                            score(k // 4, k % 4)
                        if 7 <= k < 7 + 4 * GROUP:
                            value((k - 7) // 4, (k - 7) % 4)
                        if 6 <= k < 6 + 4 * GROUP:
                            turn((k - 6) // 4, (k - 6) % 4)

                    def recur(t):
                        if t == 0:
                            pe.wait_ge(r_conved, G + 1)
                            pe.wait_ge(rw_in, 64 * (G + 1))
                            pe.wait_ge(s_taken, 4 * A + 18)
                        else:
                            pe.wait_ge(r_act, 2 * G + 1)
                        for q in range(2):
                            last = pe.matmul(ps[:, 4 + q, 0:LH], (wa, wx)[t][:], rcv[:, q * LH:(q + 1) * LH],
                                             start=True, stop=True)
                        last.then_inc(r_mm, 1)

                    def behind(first):
                        def hook(n):
                            n += first
                            if n == 8:
                                rotate(0)
                                rotate(1)
                            elif n == 9:
                                rotate(2)
                            elif n >= 11:
                                step(n - 11)
                        return hook

                    unit(V, fill, wide=True)
                    unit(V + 1, fill, wide=True, hook=behind(8))
                    unit(V + 2, fill, wide=True, hook=behind(16))
                    unit(V + 3, fill, wide=True, hook=behind(24))
                    recur(0)
                    step(21)
                    step(22)
                    recur(1)

                def c_mean():
                    pe.wait_ge(r_act, 2 * NKV * (l + 1))
                    pe.wait_ge(o_taken, 2 * NKV * (l + 1))
                    pe.wait_ge(c_taken, NKV * (l + 1))
                    sum_features(lambda d: y2[:, Y_CONV + d, :], CT, 4).then_inc(cn_mean, 1)

                def c_var():
                    pe.wait_ge(cn_sq, CT * (l + 1))
                    sum_features(lambda d: csq[:, d, :], CT, 6).then_inc(cn_mm, 1)

                unit(U + O_CG, fill, wide=True, hook=lambda n: c_mean() if n == 6 else None)
                unit(U + O_CG + 1, fill, wide=True, hook=lambda n: c_var() if n == 0 else None)
                pe.wait_ge(c_ready, CT * (l + 1))
                pe.wait_ge(cn_rt, l + 1)
                pe.wait_ge(evac, 2 * (U + O_PW))
                for t in range(CT):
                    pe.wait_ge(lo_ready, 4 * (U + O_PW) + t + 1)
                    for k in range(CT):
                        for q in range(2):
                            tok = slice(q * LH, (q + 1) * LH)
                            dst = ps[:, 2 * t + q, 0:LH]
                            first = pe.matmul(dst, wh[:, t, k, 0:P], chi[:, k, tok], start=(k == 0), stop=False)
                            if t == k == q == 0:
                                first.then_inc(pass0_done, 1)
                            pe.matmul(dst, wh[:, t, k, 0:P], clo[:, k, tok], start=False, stop=False)
                            last = pe.matmul(dst, wl[:, t, k, 0:P], chi[:, k, tok], start=False, stop=(k == CT - 1))
                    last.then_inc(piece_used, 1)
                with pe.Fori(0, 8) as d:
                    unit(U + O_OUT + d, fill + KT, wide=True)
            norm(LAYERS)

            for q in range(4):
                for k in range(4):
                    d = 4 * q + k
                    pe.wait_ge(y_full, LAYERS * KT + d + 1)
                    if k == 0 and q >= 2:
                        pe.wait_ge(fin_act, 2 * q - 2)
                        pe.wait_ge(fin_dve, 2 * q - 2)
                    for i in range(ST):
                        last = pe.transpose(ps[:, 4 * (q % 2) + i, k * P:(k + 1) * P], y2[:, d, NM + i * P:NM + (i + 1) * P], ident[:])
                last.then_inc(fin_tr, 1)

        @block.scalar
        def _(act):
            def high(U, j):
                act.wait_ge(raw_full[j], 32 * U + 32)
                if not (isinstance(U, int) and U == 0):
                    act.wait_ge(piece_used, 4 * U - 3 + j)
                act.activation(wh[:, j], raw[:, j], ACT.Copy).then_inc(hi_ready, 1)

            def passed(U, m):
                if m == 0:
                    act.wait_ge(pass0_done, U + 1)
                else:
                    act.wait_ge(piece_used, 4 * U + 4)

            def take(U, m, dst, src, fn=ACT.Copy, **kw):
                passed(U, m)
                act.activation(dst, src, fn, **kw).then_inc(evac, 1)

            act.wait_ge(xn_in, 16 * ST)
            for i in range(ST):
                act.activation(xs[:, i, :], xn[:, i, :], ACT.Square, accum_out=small[:, i:i + 1])
                act.drain()
            act.sem_inc(x_ss, 1)
            act.wait_ge(x_var, 1)
            act.activation(small[:, 8:12], small[:, 4:8], ACT.Sqrt).then_inc(x_sd, 1)
            for j in range(4):
                high(0, j)
            act.wait_ge(par_tr, 1)
            act.activation(par[:, 0, :], ps[:, 0, 0:P], ACT.Copy)
            act.activation(par[:, 1, 0:ROWS1], ps[:, 1, 0:ROWS1], ACT.Copy).then_inc(par_ok, 1)
            act.drain()
            for d in range(KT):
                act.wait_ge(tr_sc, d + 1)
                act.activation(xh[:, d, 0:S], ps[:, 4 + d % 4, :], ACT.Copy, scale=par[:, 0, PR_NORM + d:PR_NORM + d + 1])\
                   .then_inc(xh_done, 1)

            take(0, 0, li[:], ps[0:H, 0, :], ACT.Identity, bias=small[0:H, 60:61])
            for j in range(4):
                high(1, j)
            take(0, 1, xf[:], ps[0:H, 1, :], ACT.Identity, bias=small[0:H, 61:62])
            act.wait_ge(wst_tr, 1)
            act.activation(wst[:].rearrange("p h t -> p (h t)"), ps[:, 4:6, :].rearrange("p a n -> p (a n)"), ACT.Copy)\
               .then_inc(wst_ok, 1)
            act.drain()
            act.activation(gz[:], xf[:], ACT.Abs)
            act.drain()
            act.activation(gz[:], gz[:], ACT.Exp, scale=-1.0).then_inc(g_z, 1)
            act.wait_ge(rs_mm, 1)
            act.activation(rsb[:].rearrange("p h t -> p (h t)"), ps[:, 6:8, :].rearrange("p a n -> p (a n)"), ACT.Copy)\
               .then_inc(rs_ok, 1)
            act.wait_ge(g_m, 1)
            act.activation(gout[:, 1, :], gq[:], ACT.Exp, scale=-1.0).then_inc(g_em, 1)

            with act.Fori(0, H) as h:
                U = U_SGU + 3 * h
                act.wait_ge(vn_ready, h)
                for m in range(2):
                    take(U, m, vg[:, 2 * m:2 * m + 2, :], ps[:, m, :].rearrange("p (a n) -> p a n", a=2), ACT.Gelu_apprx_tanh)
                    if m == 0:
                        for j in range(4):
                            high(U + 1, j)
                act.wait_ge(a_var, h + 1)
                act.activation(small[:, 52:56], small[:, 48:52], ACT.Sqrt).then_inc(a_sd, 1)
                act.wait_ge(ug_used, h)
                for m in range(2):
                    take(U + 1, m, ug[:, m, :], ps[:, m, :], ACT.Gelu_apprx_tanh)
                    if m == 0:
                        for j in range(4):
                            high(U + 2, j)
                act.wait_ge(yg_done, h)
                for m in range(2):
                    take(U + 2, m, zg[:, m, :], ps[:, m, :], ACT.Silu)
                    if m == 0:
                        for j in range(4):
                            high(U + 3, j)

            act.wait_ge(at_tr, 1)
            act.activation(at[:].rearrange("p i h -> p (i h)"), ps[:, 6, 0:ST * H], ACT.Copy).then_inc(at_ok, 1)
            act.wait_ge(yg_done, H)
            act.drain()

            with act.Fori(0, H) as h:
                U = U_MLSTM + 4 * h

                def silu(t, n, col):
                    act.wait_ge(cq_done, 2 * h + n)
                    act.activation(t[:], t[:], ACT.Silu, bias=par[:, 0, ds(col + h, 1)]).then_inc(qk_ready, 1)

                act.wait_ge(ym_done, h + 1)
                take(U, 0, cr[:, 3:3 + S], ps[:, 0, :])
                silu(qc, 1, PR_CONVB)
                for j in range(4):
                    high(U + 1, j)
                take(U, 1, cr[:, 3:3 + S], ps[:, 1, :])
                silu(kc, 2, PR_CONVB + H)
                act.wait_ge(pv_m, h)
                take(U + 1, 0, vv[:, 0:2, :], ps[:, 0, :].rearrange("p (a n) -> p a n", a=2))
                for j in range(ST):
                    act.wait_ge(p_arg, ST * h + j + 1)
                    pjj = pj[:, shift[j]:shift[j] + S - j * P]
                    act.activation(pjj, pjj, ACT.Exp).then_inc(p_exp, 1)
                for j in range(4):
                    high(U + 2, j)
                take(U + 1, 1, vv[:, 2:4, :], ps[:, 1, :].rearrange("p (a n) -> p a n", a=2))
                take(U + 2, 0, og[:, 0, :], ps[:, 0, :], ACT.Sigmoid)
                high(U + 3, 0)
                act.wait_ge(pv_m, h + 1)
                act.activation(rd[:], ps[:, 6, :], ACT.Abs).then_inc(den_abs, 1)
                for j in range(1, 4):
                    high(U + 3, j)
                act.wait_ge(h_ready, h + 1)
                act.activation(sq[:], ym[:, ds(2 * h, 2), :], ACT.Square).then_inc(sq_ready, 1)
                take(U + 2, 1, og[:, 1, :], ps[:, 1, :], ACT.Sigmoid)
                act.wait_ge(zz_used, 2 * h)
                take(U + 3, 0, zz[:], ps[:, 0, :], ACT.Silu)
                act.wait_ge(ms_mm, h + 1)
                act.activation(rd[:], ps[:, 7, :], ACT.Sqrt, scale=1.0 / DV, bias=small[:, 62:63]).then_inc(rms_rt, 1)
                for j in range(4):
                    high(U + 4, j)
                act.wait_ge(zz_used, 2 * h + 1)
                take(U + 3, 1, zz[:], ps[:, 1, :], ACT.Silu)

            def fill_piece(j, src, wide):
                for k in (4 * j, 4 * j + 2):
                    act.activation(xh[:, k:k + 2, 0:wide], src[:, k:k + 2, 0:wide], ACT.Copy).then_inc(xh_done, 2)

            act.wait_ge(ym_done, H + 1)
            act.wait_ge(piece_used, 4 * U_OUT_M)
            for j in range(4):
                fill_piece(j, ym, S)
            for half_, U0 in ((0, U_OUT_M), (1, U_OUT_G)):
                with act.Fori(0, 7) as d:
                    for m in range(2):
                        act.wait_ge(tmp_used, 16 * half_ + 2 * d + m + 1)
                        take(U0 + d, m, tmp[:, m, :], ps[:, m, :])
                        if m == 0:
                            for j in range(4):
                                high(U0 + d + 1, j)
                act.wait_ge(tmp_used, 16 * half_ + 15)
                take(U0 + 7, 0, tmp[:, 0, :], ps[:, 0, :])
                if half_ == 0:
                    for j in range(4):
                        high(U_OUT_G, j)
                        fill_piece(j, yg, S)
                act.wait_ge(tmp_used, 16 * half_ + 16)
                take(U0 + 7, 1, tmp[:, 1, :], ps[:, 1, :])
                if half_ == 0:
                    act.wait_ge(meta_tr, 1)
                    act.wait_ge(x_ready, 3 * KT)
                    act.drain()
                    act.activation(res[:, :, 0:NM], ps[:, 5, 0:KT * NM].rearrange("p (d n) -> p d n", n=NM), ACT.Copy)\
                       .then_inc(meta_ok, 1)

            def norm(n, U=None):
                eps = small[:, 59:60]
                act.activation(small[:, 58:59], small[:, 63:64], ACT.Sqrt)
                act.wait_ge(ln_mean, n + 1)
                act.activation(two(mub[:]), halves(4), ACT.Copy, scale=1.0 / P).then_inc(mu_ok, 1)
                if U is not None:
                    high(U, 0)
                act.wait_ge(ln_mm, n + 1)
                act.activation(two(lrb[:]), halves(6), ACT.Sqrt, scale=1.0 / D, bias=eps).then_inc(ln_rt, 1)
                if U is not None:
                    for j in range(1, 4):
                        high(U, j)
                for d in range(KT):
                    act.wait_ge(ln_t, KT * n + d + 1)
                    act.activation(y2[:, d, :], res[:, d, :], ACT.Identity, bias=plc(PL_PB + d)).then_inc(y_full, 1)
                    if U is not None:
                        act.drain()
                        act.activation(xh[:, d, :], y2[:, d, :], ACT.Copy).then_inc(xh_done, 1)

            with act.Fori(0, LAYERS) as l:
                U = U_LAYER + N_LAYER * l
                norm(l, U)
                act.wait_ge(x_ready, 4 * KT + 2 * KT * l)
                act.dma_start(x_res, y2[:]).then_inc(res_out, 16)
                act.dma_start(kshape[:], consts[:, K_ROT:K_ALL]).then_inc(shape_in, 16)
                row = 0
                for name, n in (("conv_dw_w_2", TAPS * CT), ("conv_dw_b_2", CT), ("conv_ln_g_2", CT), ("conv_ln_b_2", CT),
                                ("conv_pw_b_2", CT), ("lru_conv_w_2", RTAPS * CT), ("lru_conv_b_2", CT), ("ln_post_g_2", KT),
                                ("ln_post_b_2", KT), ("lru_ba_2", CT), ("lru_bx_2", CT), ("lru_lambda_2", CT)):
                    v = a[name]
                    v = (v.rearrange("l j (t p) -> l (j t) p", p=P) if len(v.shape) == 3
                         else v.rearrange("l (t p) -> l t p", p=P))
                    act.dma_start(prow2[row % P:row % P + n, row // P, :], v[ds(l, 1)].squeeze(0)).then_inc(pl_in, 16)
                    row += n
                act.dma_start(small[:, 0:NH], a["attn_sinks_2"][ds(l, 1)].squeeze(0).partition_broadcast(P)).then_inc(sink_in, 16)
                for m in range(2):
                    take(U + O_K, m, two(krw[:, m, :]), halves(2 * m))
                    if m == 0:
                        for j in range(4):
                            high(U + O_V, j)
                act.wait_ge(pl_tr, l + 1)
                act.activation(pl[:, 0, :], ps[:, 4, 0:P], ACT.Copy)
                act.activation(pl[:, 1, 0:ROWS_L2], ps[:, 5, 0:ROWS_L2], ACT.Copy).then_inc(pl_ok, 1)
                act.drain()
                act.activation(small[:, 41:45], plr(PL_LAM, CT), ACT.Abs)
                act.drain()
                act.activation(small[:, 41:45], small[:, 41:45], ACT.Exp, scale=-1.0).then_inc(lam_exp, 1)
                take(U + O_V, 0, v2[:, 1:1 + ST, :], ps[:, 0:2, :].rearrange("p a (b n) -> p (a b) n", b=2))
                for j in range(4):
                    high(U + O_V + 1, j)
                take(U + O_V, 1, v2[:, 0, :], ps[:, 2, 0:256])
                act.drain()
                act.wait_ge(krd_in, 128 * (l + 1))
                act.wait_ge(pads_ok, 1)

                with act.Fori(0, NKV) as g:
                    V = U + O_GRP + 4 * g
                    G = NKV * l + g
                    A = NH * l + GROUP * g

                    def exps(i):
                        act.wait_ge(att_max, A + i + 1)
                        w = NM + 2 * BLK
                        for n in range(ST):
                            p = pb[:, i % 2, n * w:n * w + (w if n else NM + BLK)]
                            act.activation(p, p, ACT.Exp, bias=small[:, 21 + n:22 + n], accum_out=small[:, 26 + n:27 + n])
                        p = pb[0:NM, i % 2, 4 * w:4 * w + NM]
                        act.activation(p, p, ACT.Exp, bias=small[0:NM, 25:26], accum_out=small[0:NM, 30:31])
                        act.activation(small[:, 31:36], small[:, 21:26], ACT.Exp,
                                       bias=small[:, ds(GROUP * g + i, 1)]).then_inc(att_exp, 1)

                    def turned(i, n):
                        act.wait_ge(pt_done, 4 * A + 4 * i + n + 1)
                        if n == 0:
                            act.activation(ptm[:], ps[0:NM, 6, 3 * BLK:3 * BLK + NM], ACT.Copy)
                        if n == 1 and i % 2:
                            act.wait_ge(o_taken, 2 * G + i // 2)
                            act.activation(mo[:], ps[:, 6, 3 * BLK + 2 * NM:3 * BLK + 3 * NM], ACT.Copy)
                        act.activation(pts[:, n % 2, :], ps[:, 6, 0:3 * BLK], ACT.Copy).then_inc(pt_evac, 1)

                    def gate(t, dst, b):
                        act.wait_ge(r_mm, 2 * G + t + 1)
                        act.activation(two(dst[:]), halves(4), ACT.Sigmoid, bias=pl[:, 1, ds(b - P + g, 1)]).then_inc(r_act, 1)

                    act.wait_ge(rope_done, 3 * G)
                    take(V, 0, two(qrw[:, 0, :]), halves(0))
                    high(V + 1, 0)
                    high(V + 1, 1)
                    high(V + 1, 2)
                    take(V, 1, two(qrw[:, 1, :]), halves(2))
                    high(V + 1, 3)
                    act.wait_ge(pv_done, A)
                    act.activation(vgr[:], v2[:, :, ds(HD * g, HD)], ACT.Copy).then_inc(vgr_ready, 1)
                    act.wait_ge(c_taken, G)
                    act.wait_ge(zeros_ok, l + 1)
                    take(V + 1, 0, two(cra[:, TAPS - 1:]), halves(0))
                    high(V + 2, 0)
                    high(V + 2, 1)
                    high(V + 2, 2)
                    exps(0)
                    act.wait_ge(o_taken, 2 * G)
                    take(V + 1, 1, two(agt[:, 0, :]), halves(2), ACT.Sigmoid)
                    high(V + 2, 3)
                    turned(0, 0)
                    turned(0, 1)
                    exps(1)
                    turned(0, 2)
                    act.wait_ge(c_gated, G + 1)
                    take(V + 2, 0, two(agt[:, 0, :]), halves(0), ACT.Silu)
                    turned(0, 3)
                    high(V + 3, 0)
                    turned(1, 0)
                    high(V + 3, 1)
                    turned(1, 1)
                    high(V + 3, 2)
                    exps(2)
                    turned(1, 2)
                    take(V + 2, 1, two(agt[:, 1, :]), halves(2), ACT.Silu)
                    high(V + 3, 3)
                    turned(1, 3)
                    turned(2, 0)
                    turned(2, 1)
                    exps(3)
                    turned(2, 2)
                    take(V + 3, 0, two(rx[:, RTAPS - 1:RTAPS - 1 + L]), halves(0))
                    turned(2, 3)
                    high(V + 4, 0)
                    turned(3, 0)
                    high(V + 4, 1)
                    turned(3, 1)
                    high(V + 4, 2)
                    act.activation(small[:, 58:59], small[:, 63:64], ACT.Sigmoid)
                    turned(3, 2)
                    gate(0, rga, PL_BA)
                    turned(3, 3)
                    high(V + 4, 3)
                    gate(1, rgx, PL_BX)
                    act.wait_ge(c_part, G + 1)
                    take(V + 3, 1, two(rgs[:]), halves(2), ACT.Silu)
                    act.drain()
                    act.activation(rth[:], rga[:], ACT.Tanh, scale=small[:, ds(49 + g, 1)])
                    act.drain()
                    act.activation(rga[:], rga[:], ACT.Exp, scale=small[:, ds(45 + g, 1)]).then_inc(r_act2, 1)
                    act.wait_ge(r_w, G + 1)
                    act.activation(rth[:], rth[:], ACT.Sqrt).then_inc(r_sqrt, 1)

                act.wait_ge(lru_done, NKV * (l + 1))
                C = U + O_CG
                take(C, 0, two(cgt[:, 0, :]), halves(0), ACT.Silu)
                for j in range(3):
                    high(C + 1, j)
                for d in range(CT):
                    act.wait_ge(cn_c, CT * l + d + 1)
                    act.activation(csq[:, d, :], y2[:, Y_CONV + d, :], ACT.Square).then_inc(cn_sq, 1)
                high(C + 1, 3)
                take(C, 1, two(cgt[:, 1, :]), halves(2), ACT.Silu)
                act.wait_ge(cn_mm, l + 1)
                act.activation(two(lrb[:]), halves(6), ACT.Sqrt, scale=1.0 / CW, bias=small[:, 63:64]).then_inc(cn_rt, 1)
                for d in range(CT):
                    act.wait_ge(cn_t, CT * l + d + 1)
                    act.activation(y2[:, Y_CONV + d, :], y2[:, Y_CONV + d, :], ACT.Silu, bias=pl[:, 1, PL_CLB - P + d:PL_CLB - P + d + 1])
                    act.drain()
                    act.activation(chi[:, d, :], y2[:, Y_CONV + d, :], ACT.Copy).then_inc(cn_hi, 1)
                take(C + 1, 0, two(cgt[:, 2, :]), halves(0), ACT.Silu)
                for j in range(4):
                    high(C + 2, j)
                    if j < 3:
                        fill_piece(j, y2, L)
                take(C + 1, 1, two(cgt[:, 3, :]), halves(2), ACT.Silu)
                act.wait_ge(c_ready, CT * (l + 1))
                W = U + O_PW
                for t in range(CT):
                    act.wait_ge(piece_used, 4 * W + t + 1)
                    ins = act.activation(two(y2[:, Y_CONV + t, :]), halves(2 * t), ACT.Identity,
                                         bias=pl[:, 1, PL_PWB - P + t:PL_PWB - P + t + 1])
                    if t % 2:
                        ins.then_inc(evac, 1)
                    act.drain()
                    act.sem_inc(pw_done, 1)
                    high(W + 1, t)
                for t in range(CT):
                    act.wait_ge(y_conv, CT * l + t + 1)
                    act.activation(xh[:, Y_CONV + t, :], y2[:, Y_CONV + t, :], ACT.Copy).then_inc(xh_done, 1)
                act.wait_ge(res_out, 16 * (l + 1))
                for c in range(4):
                    act.dma_start(res[:, 4 * c:4 * c + 4, :], x_res[:, 4 * c:4 * c + 4, :]).then_inc(res_in[c], 16)

                def out_unit(d, more):
                    for m in range(2):
                        act.wait_ge(tmp_used, 32 + KT * l + 2 * d + m + 1)
                        take(U + O_OUT + d, m, two(tmp2[:, m, :]), halves(2 * m))
                        if m == 0 and more:
                            for j in range(4):
                                high(U + O_OUT + d + 1, j)
                with act.Fori(0, 7) as d:
                    out_unit(d, True)
                out_unit(7, False)
            norm(LAYERS)

            for q in range(4):
                act.wait_ge(fin_tr, q + 1)
                for i in range(2):
                    act.activation(outn[:, q, i, :], ps[:, 4 * (q % 2) + i, :], ACT.Copy).then_inc(fin_act, 1)

        @block.vector
        def _(dve):
            def low(U, j):
                dve.wait_ge(hi_ready, 4 * U + j + 1)
                dve.tensor_tensor(wl[:, j], raw[:, j], f(wh[:, j]), ALU.subtract).then_inc(lo_ready, 1)

            def lows(U, js=range(4)):
                for j in js:
                    low(U, j)

            def log1p(w, q, p, z):
                dve.tensor_scalar(w, z, 2.0, None, ALU.add)
                dve.drain()
                dve.reciprocal(w, w)
                dve.drain()
                dve.tensor_tensor(w, w, z, ALU.mult)
                dve.drain()
                dve.tensor_tensor(q, w, w, ALU.mult)
                dve.drain()
                dve.tensor_scalar(p, q, LOG1P[8], None, ALU.mult)
                dve.drain()
                for c in LOG1P[7:0:-1]:
                    dve.scalar_tensor_tensor(p, p, c, q, ALU.add, ALU.mult)
                    dve.drain()
                dve.scalar_tensor_tensor(p, p, LOG1P[0], w, ALU.add, ALU.mult)
                dve.drain()

            dve.memset(small[:, 62:63], EPS)
            dve.memset(small[:, 63:64], LN_EPS)
            for d in range(KT):
                dve.wait_ge(tr_raw, d + 1)
                if d >= KT // 2:
                    dve.wait_ge(x_stored[d % 8], 16)
                dve.tensor_copy(stage[:, d % 8, :], ps[:, 4 + d % 4, :]).then_inc(tr_raw_free, 1)
            dve.wait_ge(x_ss, 1)
            dve.tensor_scalar(small[:, 4:8], small[:, 0:4], 1.0 / D, EPS, ALU.mult, ALU.add).then_inc(x_var, 1)
            dve.wait_ge(x_sd, 1)
            dve.reciprocal(small[:, 12:16], small[:, 8:12])
            dve.drain()
            for i in range(ST):
                last = dve.tensor_scalar(xs[:, i, :], xn[:, i, :], small[:, 12 + i:13 + i], None, ALU.mult)
            last.then_inc(xs_ready, 1)
            lows(0)
            dve.wait_ge(par_ok, 1)
            for d in range(KT):
                dve.wait_ge(xh_done, d + 1)
                dve.scalar_tensor_tensor(xl[:, d, 0:S], ps[:, 4 + d % 4, :], par[:, 0, PR_NORM + d:PR_NORM + d + 1],
                                         f(xh[:, d, 0:S]), ALU.mult, ALU.subtract).then_inc(x_ready, 1)
            lows(1)
            dve.wait_ge(g_z, 1)
            log1p(gw[:], gq[:], gp[:], gz[:])
            dve.tensor_scalar(gz[:], gp[:], -2.0, None, ALU.mult)
            dve.memset(gq[:], 0.0)
            dve.drain()
            dve.scalar_tensor_tensor(gz[:], xf[:], 0.0, gz[:], ALU.min, ALU.add)
            dve.drain()
            dve.tensor_tensor_scan(gw[:], gz[:], gq[:], 0.0, ALU.add, ALU.add)
            dve.drain()
            dve.tensor_tensor(gz[:], li[:], gw[:], ALU.subtract)
            dve.drain()
            dve.tensor_tensor_scan(gp[:], gz[:], gz[:], 0.0, ALU.max, ALU.max)
            dve.drain()
            dve.tensor_scalar(gout[:, 0, :], gp[:], -1.0, None, ALU.mult)
            dve.tensor_tensor(gq[:], gw[:], gp[:], ALU.add).then_inc(g_m, 1)
            dve.wait_ge(rs_ok, 1)
            dve.wait_ge(ws_in, 32)

            with dve.Fori(0, H) as h:
                U = U_SGU + 3 * h
                lows(U + 1)
                dve.wait_ge(evac, 2 * U + 2)
                for i in range(ST):
                    dve.bn_stats(small[:, 16 + 6 * i:22 + 6 * i], vg[:, i, :])
                dve.drain()
                for i in range(ST):
                    dve.bn_aggr(small[:, 40 + 2 * i:42 + 2 * i], small[:, 16 + 6 * i:22 + 6 * i])
                dve.drain()
                dve.tensor_scalar(small[:, 48:52].unsqueeze(2), small[:, 40:48].rearrange("p (i t) -> p i t", t=2)[:, :, 1:2], EPS, None, ALU.add)\
                   .then_inc(a_var, 1)
                dve.wait_ge(a_sd, h + 1)
                dve.reciprocal(small[:, 56:60], small[:, 52:56])
                dve.drain()
                for i in range(ST):
                    last = dve.tensor_scalar(vn[:, i, :], vg[:, i, :], small[:, 40 + 2 * i:41 + 2 * i],
                                             small[:, 56 + i:57 + i], ALU.subtract, ALU.mult)
                last.then_inc(vn_ready, 1)
                for c in range(2):
                    dve.scalar_tensor_tensor(svr[:, c, :], rsb[:, ds(h, 1), :].squeeze(1), par[:, 1, ds(PR_SGUB - P + 2 * h + c, 1)],
                                             bsp[:, ds(h, 1), :].squeeze(1), ALU.mult, ALU.add)
                dve.drain()
                dve.wait_ge(sgu_done, h + 1)
                for c in range(2):
                    last = dve.scalar_tensor_tensor(sv[:, c, :].rearrange("p (n t) -> p n t", t=P),
                                                    ps[:, 4 + c, :].rearrange("p (n t) -> p n t", t=P),
                                                    par[:, 1, ds(PR_SGUW - P + 2 * h + c, 1)],
                                                    svr[:, c:c + 1, :].broadcast_to([P, ST, P]), ALU.mult, ALU.add)
                last.then_inc(sv_done, 1)
                lows(U + 2)
                dve.drain()
                dve.wait_ge(evac, 2 * (U + 1) + 2)
                dve.tensor_tensor(sv[:], sv[:], ug[:], ALU.mult).then_inc(ug_used, 1)
                lows(U + 3)
                dve.drain()
                dve.wait_ge(evac, 2 * (U + 2) + 2)
                dve.tensor_tensor(yg[:, ds(2 * h, 2), :], sv[:], zg[:], ALU.mult).then_inc(yg_done, 1)

            dve.drain()
            dve.memset(cr[:, 0:3], 0.0).then_inc(ym_done, 1)

            with dve.Fori(0, H) as h:
                U = U_MLSTM + 4 * h

                def conv(dst, col):
                    dve.tensor_scalar(dst[:], cr[:, 0:S], par[:, 0, ds(PR_CONVW + col + h, 1)], None, ALU.mult)
                    dve.drain()
                    for j in range(1, 4):
                        ins = dve.scalar_tensor_tensor(dst[:], cr[:, j:j + S], par[:, 0, ds(PR_CONVW + 16 * j + col + h, 1)],
                                                       dst[:], ALU.mult, ALU.add)
                        if j < 3:
                            dve.drain()
                    ins.then_inc(cq_done, 1)

                dve.wait_ge(evac, 2 * U + 1)
                dve.wait_ge(s_mm, ST * h)
                conv(qc, 0)
                lows(U + 1)
                dve.wait_ge(evac, 2 * U + 2)
                conv(kc, H)
                dve.wait_ge(bc_in, 16 * h + 16)
                dve.wait_ge(at_ok, 1)
                dve.wait_ge(ms_mm, h)
                for j in range(ST):
                    dve.tensor_scalar(pj[:, shift[j]:shift[j] + S - j * P], bc[:, 0, j * P:S], at[:, j, ds(h, 1)], 0.0,
                                      ALU.add, ALU.min).then_inc(p_arg, 1)
                for j in range(ST):
                    dve.wait_ge(p_exp, ST * h + j + 1)
                    dve.wait_ge(s_mm, ST * h + j + 1)
                    pjj = pj[:, shift[j]:shift[j] + S - j * P]
                    dve.scalar_tensor_tensor(pjj, ps[:, 4 + j, 0:S - j * P], float(P) ** -0.5, pjj, ALU.mult, ALU.mult)
                    dve.drain()
                    dve.tensor_tensor(pjj[:, 0:P], pjj[:, 0:P], tri[:], ALU.mult).then_inc(p_done, 1)
                lows(U + 2)
                low(U + 3, 0)
                dve.wait_ge(den_abs, h + 1)
                dve.tensor_tensor(rd[:], rd[:], bc[:, 1, :], ALU.max)
                dve.drain()
                dve.reciprocal(rd[:], rd[:])
                dve.drain()
                last = dve.tensor_tensor(ym[:, ds(2 * h, 2), :], ps[:, 4:6, :], rd[:].unsqueeze(1).broadcast_to([P, 2, S]), ALU.mult)
                last.then_inc(h_ready, 1)
                lows(U + 3, range(1, 4))
                dve.wait_ge(evac, 2 * (U + 3) + 1)
                dve.tensor_tensor(og[:, 0, :], og[:, 0, :], zz[:], ALU.mult).then_inc(zz_used, 1)
                dve.wait_ge(rms_rt, h + 1)
                dve.reciprocal(rd[:], rd[:])
                dve.drain()
                dve.tensor_tensor(ym[:, ds(2 * h, 2), :], ym[:, ds(2 * h, 2), :], rd[:].unsqueeze(1).broadcast_to([P, 2, S]), ALU.mult)
                lows(U + 4)
                dve.wait_ge(evac, 2 * (U + 3) + 2)
                dve.tensor_tensor(og[:, 1, :], og[:, 1, :], zz[:], ALU.mult).then_inc(zz_used, 1)
                dve.drain()
                dve.memset(cr[:, 0:3], 0.0)
                dve.drain()
                for c in range(2):
                    y = ym[:, ds(2 * h + c, 1), :].squeeze(1)
                    last = dve.scalar_tensor_tensor(y, y, par[:, 0, ds(PR_MNORM + 2 * h + c, 1)], og[:, c, :], ALU.mult, ALU.mult)
                last.then_inc(ym_done, 1)

            def fill_piece(j, src, wide, base):
                for k in (4 * j, 4 * j + 2):
                    dve.wait_ge(xh_done, base + k + 2)
                    dve.tensor_tensor(xl[:, k:k + 2, 0:wide], src[:, k:k + 2, 0:wide], f(xh[:, k:k + 2, 0:wide]), ALU.subtract)\
                       .then_inc(x_ready, 2)

            def spread(k):
                dve.drain()
                dve.tensor_tensor(dif[:], k, res[:, 0, :], ALU.subtract)
                dve.drain()
                dve.tensor_tensor(dsum[:], dsum[:], dif[:], ALU.add)
                dve.tensor_tensor(dsq[:], dif[:], dif[:], ALU.mult)
                dve.drain()
                dve.tensor_tensor(dsqs[:], dsqs[:], dsq[:], ALU.add)

            dve.drain()
            dve.memset(small[:, 59:60], LN_EPS * EPS).then_inc(tmp_used, 2)
            for j in range(4):
                fill_piece(j, ym, S, KT)
            dve.memset(dsum[:], 0.0)
            dve.memset(dsqs[:], 0.0)
            dve.memset(ssum[:, NM:L], 0.0)
            dve.memset(ssum[:, 0:NM], (1.0 - EPS) * D / P)
            for half_, U0 in ((0, U_OUT_M), (1, U_OUT_G)):
                def add(d, m):
                    k = 2 * d + m
                    dve.wait_ge(evac, 2 * (U0 + d) + m + 1)
                    dst = acc[:, ds(k, 1), :].squeeze(1)
                    dve.tensor_tensor(dst, dst, tmp[:, m, :], ALU.add).then_inc(tmp_used, 1)
                    if half_:
                        dve.drain()
                        r = res[:, ds(k, 1), :].squeeze(1)
                        dve.tensor_scalar(r[:, NM:L], dst, par[:, 0, ds(PR_FINAL + k, 1)], None, ALU.mult)
                        dve.tensor_tensor(dsq[:, NM:L], dst, dst, ALU.mult)
                        dve.drain()
                        dve.tensor_tensor(ssum[:, NM:L], ssum[:, NM:L], dsq[:, NM:L], ALU.add)
                        spread(r)
                if half_ == 0:
                    dve.wait_ge(acc_in, 16)
                else:
                    dve.wait_ge(meta_ok, 1)
                lows(U0 + 1)
                for m in range(2):
                    add(0, m)
                with dve.Fori(1, 7) as d:
                    lows(U0 + d + 1)
                    for m in range(2):
                        add(d, m)
                if half_ == 0:
                    for j in range(4):
                        low(U_OUT_G, j)
                        fill_piece(j, yg, S, 2 * KT)
                for m in range(2):
                    add(7, m)

            def norm(n, U=None):
                dve.drain()
                dve.scalar_tensor_tensor(dif[:], dsum[:], 1.0 / KT, res[:, 0, :], ALU.mult, ALU.add).then_inc(ln_local, 1)
                dve.tensor_tensor(dsq[:], dsum[:], dsum[:], ALU.mult)
                dve.drain()
                dve.scalar_tensor_tensor(dsqs[:], dsq[:], -1.0 / KT, dsqs[:], ALU.mult, ALU.add)
                if U is not None:
                    dve.drain()
                    dve.scalar_tensor_tensor(dsqs[:], ssum[:], LN_EPS, dsqs[:], ALU.mult, ALU.add)
                dve.drain()
                dve.wait_ge(mu_ok, n + 1)
                dve.tensor_tensor(dif[:], dif[:], mub[:], ALU.subtract)
                dve.drain()
                dve.scalar_tensor_tensor(dsq[:], dif[:], float(KT), dif[:], ALU.mult, ALU.mult)
                dve.drain()
                dve.tensor_tensor(dsqs[:], dsqs[:], dsq[:], ALU.add).then_inc(ln_m2, 1)
                if U is not None:
                    low(U, 0)
                dve.drain()
                dve.wait_ge(ln_rt, n + 1)
                dve.reciprocal(lrb[:], lrb[:])
                dve.drain()
                for d in range(KT + 2 if U is not None else KT):
                    if d < KT:
                        dve.wait_ge(ln_sub, KT * n + d + 1)
                        dve.scalar_tensor_tensor(res[:, d, :], res[:, d, :], plc(PL_PG + d), lrb[:], ALU.mult, ALU.mult).then_inc(ln_t, 1)
                    if U is not None and d in (4, 6, 8):
                        low(U, d // 2 - 1)
                    if U is not None and d >= 2:
                        e = d - 2
                        dve.wait_ge(xh_done, norm_fill(n) + e + 1)
                        dve.tensor_tensor(xl[:, e, :], y2[:, e, :], f(xh[:, e, :]), ALU.subtract).then_inc(x_ready, 1)

            norm_fill = lambda n: (3 + 2 * n) * KT

            dve.drain()
            dve.memset(small[:, 16:41], 1.0)
            dve.memset(wa[:], 0.0)
            dve.memset(wx[:], 0.0)
            dve.drain()
            dve.sem_inc(pads_ok, 1)
            dve.sem_inc(s_taken, 2)

            with dve.Fori(0, LAYERS) as l:
                U = U_LAYER + N_LAYER * l
                norm(l, U)
                dve.drain()
                dve.memset(small[:, 59:60], LN_EPS)
                dve.drain()
                lows(U + O_V)
                dve.memset(cra[:, 0:TAPS - 1], 0.0)
                dve.memset(rx[:, 0:RTAPS - 1], 0.0).then_inc(zeros_ok, 1)
                dve.wait_ge(lam_exp, l + 1)
                z, w, q, p = small[:, 41:45], small[:, 45:49], small[:, 49:53], small[:, 53:57]
                log1p(w, q, p, z)
                dve.tensor_scalar(z, plr(PL_LAM, CT), -1.0, 0.0, ALU.mult, ALU.max)
                dve.drain()
                dve.scalar_tensor_tensor(z, p, 2.0, z, ALU.mult, ALU.add)
                dve.drain()
                dve.tensor_scalar(w, z, -8.0, None, ALU.mult)
                dve.tensor_scalar(q, z, 8.0, None, ALU.mult).then_inc(sp_ok, 1)
                dve.wait_ge(shape_in, 16 * (l + 1))
                dve.wait_ge(sink_in, 16 * (l + 1))
                dve.wait_ge(res_out, 16 * (l + 1))
                lows(U + O_V + 1)

                with dve.Fori(0, NKV) as g:
                    V = U + O_GRP + 4 * g
                    G = NKV * l + g
                    A = NH * l + GROUP * g
                    W3 = NM + 2 * BLK

                    def scored(i, n):
                        dve.wait_ge(s_done, 4 * A + 4 * i + n + 1)
                        w = W3 if n else NM + BLK
                        ins = dve.scalar_tensor_tensor(pb[:, i % 2, n * W3:n * W3 + w], ps[:, 4 + n % 2, 0:w],
                                                       float(HD) ** -0.5, mas if n else ma0, ALU.mult, ALU.add)
                        if n == 0:
                            ins = dve.scalar_tensor_tensor(pb[0:NM, i % 2, 4 * W3:4 * W3 + NM], ps[0:NM, 4, 160:160 + NM],
                                                           float(HD) ** -0.5, mca[0:NM, :], ALU.mult, ALU.add)
                        ins.then_inc(s_taken, 1)
                        if n == 3:
                            dve.drain()
                            dve.tensor_reduce(small[:, 16:17], pb[:, i % 2, 0:NM + BLK], AX.X, ALU.max)
                            dve.tensor_reduce(small[:, 17:20], pb[:, i % 2, W3:4 * W3].rearrange("p (n w) -> p n w", w=W3), AX.X, ALU.max)
                            dve.tensor_reduce(small[0:NM, 20:21], pb[0:NM, i % 2, 4 * W3:4 * W3 + NM], AX.X, ALU.max)
                            dve.drain()
                            dve.tensor_scalar(small[:, 21:26], small[:, 16:21], small[:, ds(GROUP * g + i, 1)], -1.0,
                                              ALU.max, ALU.mult).then_inc(att_max, 1)

                    def summed(i):
                        dve.wait_ge(att_exp, A + i + 1)
                        dve.tensor_tensor(small[:, 36:41], small[:, 26:31], small[:, 31:36], ALU.add)
                        dve.drain()
                        dve.reciprocal(small[:, 36:41], small[:, 36:41]).then_inc(att_sum, 1)

                    def taps(a0, a1):
                        dve.drain()
                        if a0 == PTAPS:
                            dve.wait_ge(c_gated, G + 1)
                        for j in range(a0, a1):
                            wj = pl[:, 0, ds(CT * j + g, 1)]
                            if j == PTAPS:
                                dve.tensor_scalar(cacc[:], cra[:, j:j + L], wj, pl[:, 0, ds(PL_DWB + g, 1)], ALU.mult, ALU.add)
                            else:
                                dve.scalar_tensor_tensor(cacc[:], cra[:, j:j + L], wj, cacc[:], ALU.mult, ALU.add)
                            dve.drain()

                    def attended(c):
                        dve.wait_ge(pv_done, A + 2 * c + 2)
                        dve.wait_ge(evac, 2 * (V + 2) + c + 1)
                        y = y2[:, ds(Y_ATT + 2 * g + c, 1), :].squeeze(1)
                        dve.tensor_tensor(y[:, NM:L], ps[:, 7, :], agt[:, c, NM:L], ALU.mult)
                        dve.tensor_tensor(y[:, 0:NM], mo[:], agt[:, c, 0:NM], ALU.mult)\
                           .then_inc(o_taken, 1)

                    def rope(t):
                        src = qrw[:, t, :] if t < 2 else krd[:, ds(g, 1), :].squeeze(1)
                        dst = qg[:, t, :] if t < 2 else kg[:]
                        dve.drain()
                        dve.wait_ge(rot_mm, 3 * G + t + 1)
                        dve.tensor_tensor(two(t1[:]), halves(4 + 2 * (t % 2)), two(sin), ALU.mult)
                        dve.tensor_tensor(dst, src, cos, ALU.mult)
                        dve.drain()
                        dve.tensor_tensor(dst, dst, t1[:], ALU.add).then_inc(rope_done, 1)

                    lows(V + 1)
                    rope(0)
                    rope(1)
                    rope(2)
                    scored(0, 0)
                    scored(0, 1)
                    low(V + 2, 0)
                    scored(0, 2)
                    low(V + 2, 1)
                    scored(0, 3)
                    low(V + 2, 2)
                    scored(1, 0)
                    summed(0)
                    low(V + 2, 3)
                    scored(1, 1)
                    taps(PTAPS, 11)
                    scored(1, 2)
                    taps(11, 12)
                    scored(1, 3)
                    taps(12, 13)
                    scored(2, 0)
                    summed(1)
                    scored(2, 1)
                    low(V + 3, 0)
                    scored(2, 2)
                    low(V + 3, 1)
                    taps(13, 14)
                    scored(2, 3)
                    low(V + 3, 2)
                    scored(3, 0)
                    summed(2)
                    low(V + 3, 3)
                    scored(3, 1)
                    taps(14, 15)
                    scored(3, 2)
                    attended(0)
                    taps(15, 16)
                    scored(3, 3)
                    taps(16, 17)
                    summed(3)
                    dve.drain()
                    dve.wait_ge(pt_done, 4 * A + 12)
                    dve.wait_ge(evac, 2 * (V + 3) + 1)
                    rwc = lambda j: pl[:, 1, ds(PL_RW - P + CT * j + g, 1)]
                    dve.tensor_scalar(rcv[:], rx[:, 0:L], rwc(0), pl[:, 1, ds(PL_RB - P + g, 1)], ALU.mult, ALU.add)
                    for j in range(1, RTAPS):
                        dve.drain()
                        ins = dve.scalar_tensor_tensor(rcv[:], rx[:, j:j + L], rwc(j), rcv[:], ALU.mult, ALU.add)
                    ins.then_inc(r_conved, 1)
                    low(V + 4, 0)
                    taps(17, 18)
                    low(V + 4, 1)
                    taps(18, 19)
                    low(V + 4, 2)
                    taps(19, 20)
                    low(V + 4, 3)
                    attended(1)
                    taps(20, 22)
                    dve.drain()
                    dve.wait_ge(r_act2, G + 1)
                    dve.tensor_tensor(rcv[:], rcv[:], rgx[:], ALU.mult)
                    dve.drain()
                    dve.tensor_tensor(rgx[:], rga[:], rga[:], ALU.mult)
                    dve.drain()
                    dve.scalar_tensor_tensor(rth[:], rgx[:], 1.0, rth[:], ALU.add, ALU.mult).then_inc(r_w, 1)
                    taps(22, 24)
                    dve.wait_ge(r_sqrt, G + 1)
                    dve.tensor_tensor(rcv[:], rcv[:], rth[:], ALU.mult)
                    dve.drain()
                    dve.tensor_tensor_scan(rth[:], rga[:], rcv[:], 0.0, ALU.mult, ALU.add)
                    dve.drain()
                    dve.wait_ge(evac, 2 * (V + 3) + 2)
                    dve.tensor_tensor(y2[:, ds(Y_LRU + g, 1), :].squeeze(1), rth[:], rgs[:], ALU.mult).then_inc(lru_done, 1)
                    taps(24, TAPS)
                    dve.wait_ge(c_part, G + 1)
                    ct = y2[:, ds(Y_CONV + g, 1), :].squeeze(1)
                    dve.tensor_tensor(ct, ct, cacc[:], ALU.add).then_inc(c_taken, 1)

                C = U + O_CG
                yc = lambda d: y2[:, Y_CONV + d, :]
                dve.drain()
                lows(C + 1, range(3))
                dve.wait_ge(cn_mean, l + 1)
                for d in range(CT):
                    dve.scalar_tensor_tensor(two(yc(d)), halves(4), -1.0 / CW, two(yc(d)), ALU.mult, ALU.add).then_inc(cn_c, 1)
                low(C + 1, 3)
                dve.wait_ge(cn_rt, l + 1)
                dve.reciprocal(lrb[:], lrb[:])
                dve.drain()
                for d in range(CT):
                    dve.scalar_tensor_tensor(yc(d), yc(d), plc(PL_CLG + d), lrb[:], ALU.mult, ALU.mult).then_inc(cn_t, 1)
                for d in range(CT):
                    dve.wait_ge(cn_hi, CT * l + d + 1)
                    dve.tensor_tensor(clo[:, d, :], yc(d), f(chi[:, d, :]), ALU.subtract).then_inc(c_ready, 1)
                for j in range(4):
                    low(C + 2, j)
                    if j < 3:
                        fill_piece(j, y2, L, norm_fill(l) + KT)
                W = U + O_PW
                dve.memset(dsum[:], 0.0)
                dve.memset(dsqs[:], 0.0)
                dve.memset(ssum[:], 0.0)
                for t in range(CT):
                    dve.wait_ge(pw_done, CT * l + t + 1)
                    if t == CT - 1:
                        dve.wait_ge(evac, 2 * (C + 1) + 2)
                    dve.tensor_tensor(yc(t), yc(t), cgt[:, t, :], ALU.mult).then_inc(y_conv, 1)
                    low(W + 1, t)
                for t in range(CT):
                    dve.wait_ge(xh_done, norm_fill(l) + KT + Y_CONV + t + 1)
                    dve.tensor_tensor(xl[:, Y_CONV + t, :], yc(t), f(xh[:, Y_CONV + t, :]), ALU.subtract).then_inc(x_ready, 1)

                def add(d, m):
                    dve.wait_ge(evac, 2 * (U + O_OUT + d) + m + 1)
                    dst = res[:, ds(2 * d + m, 1), :].squeeze(1)
                    dve.scalar_tensor_tensor(dst, dst, ALPHA, tmp2[:, m, :], ALU.mult, ALU.add).then_inc(tmp_used, 1)
                    spread(dst)
                for c in range(4):
                    dve.wait_ge(res_in[c], 16 * (l + 1))
                lows(W + 2)
                for m in range(2):
                    add(0, m)
                with dve.Fori(1, 7) as d:
                    lows(U + O_OUT + d + 1)
                    for m in range(2):
                        add(d, m)
                for m in range(2):
                    add(7, m)
            norm(LAYERS)

            for q in range(4):
                dve.wait_ge(fin_tr, q + 1)
                for i in range(2, 4):
                    dve.tensor_copy(outn[:, q, i, :], ps[:, 4 * (q % 2) + i, :]).then_inc(fin_dve, 1)


def shape_constants():
    c = np.zeros((P, K_ALL), np.float32)
    i = np.arange(P)
    c[:, K_IDENT:K_IDENT + P] = np.eye(P)
    c[:, K_ONES:K_ONES + P] = 1.0
    c[:, K_TRI:K_TRI + P] = i[:, None] <= i[None, :]
    half = HD // 4 // 2
    for o in (0, HD):
        for d in range(half):
            c[o + half + d, K_ROT + o + d] = -1.0
            c[o + d, K_ROT + o + half + d] = 1.0
    neg = np.float32(-1e30)
    own = np.where(i[None, :] <= i[:, None], np.float32(0), neg)
    prev = np.where(i[None, :] > i[:, None], np.float32(0), neg)
    c[:, K_MASK0 + NM:K_MASK] = own
    c[:, K_MASK + NM:K_MASK + NM + BLK] = prev
    c[:, K_MASK + NM + BLK:K_CAUS] = own
    c[:, K_CAUS:K_COS] = own[:, 0:NM]
    freq = np.float32(500000.0) ** (-np.arange(half, dtype=np.float32) / np.float32(half))
    ang = np.arange(L, dtype=np.float32)[:, None] * freq.astype(np.float32)[None, :]
    c[:, K_COS:K_SIN] = 1.0
    for o in (0, HD):
        for q in (0, half):
            c[o + q:o + q + half, K_COS:K_SIN] = np.cos(ang).T
            c[o + q:o + q + half, K_SIN:K_ALL] = np.sin(ang).T
    return c


NAMES = ["x", "norm_w", "w_in", "conv_w", "conv_b", "b_igate", "b_fgate", "mlstm_norm_w", "sgu_norm_w", "sgu_norm_b",
         "w_spatial", "b_spatial", "w_out", "final_norm_w", "meta_tokens_2", "ln_in_g_2", "ln_in_b_2", "w_in_2",
         "conv_dw_w_2", "conv_dw_b_2", "conv_ln_g_2", "conv_ln_b_2", "conv_pw_w_2", "conv_pw_b_2", "attn_sinks_2",
         "lru_conv_w_2", "lru_conv_b_2", "lru_wa_2", "lru_ba_2", "lru_wx_2", "lru_bx_2", "lru_lambda_2", "w_out_2",
         "ln_post_g_2", "ln_post_b_2"]


def kernel(**inputs):
    import concourse.bacc as bacc
    from concourse.bass_utils import run_bass_kernel_spmd

    nc = bacc.Bacc("TRN2", target_bir_lowering=False, num_devices=1)
    arrays, aps = {}, {}
    for name in NAMES + ["shape_constants"]:
        v = shape_constants() if name == "shape_constants" else np.ascontiguousarray(inputs[name])
        arrays[f"in_{name}"] = v
        aps[name] = nc.dram_tensor(f"in_{name}", v.shape, mybir.dt.from_np(v.dtype), kind="ExternalInput").ap()
    out = nc.dram_tensor("out", (1, S, D), F32, kind="ExternalOutput").ap()
    program(nc, aps, out)
    return run_bass_kernel_spmd(nc, [arrays], core_ids=[0]).results[0]["out"]
```
